# Optimizing a Trainium2 kernel written in Bass

```python
import jax, jax.numpy as jnp
from jax import lax
import numpy as np

D_MODEL = 1024
BATCH = 1
SEQ = 512
DEPTH = 2

GRID_W = 64
CTX_LEN = 256
N_HEADS = 8
QK_NOPE = 128
QK_ROPE = 64
V_DIM = 128
Q_LORA = 256
KV_LORA = 128
POOL_W = 512
POOL_WINDOWS = (2, 4, 8, 16)
N_POOL_GROUPS = 4
POOL_GROUP = POOL_W // N_POOL_GROUPS
D_FF = -(-8 * D_MODEL // (3 * 256)) * 256
N_BRANCH = 2
N_MOD = 6
ROPE_THETA = 10000.0
ROPE_AXIS = QK_ROPE // 2
EPS = 1e-6
Q_BLOCK = 128
ATTN_SCALE = (QK_NOPE + QK_ROPE) ** -0.5

OFF_KV = Q_LORA
OFF_KR = OFF_KV + KV_LORA
OFF_POOL = OFF_KR + QK_ROPE
OFF_GATE = OFF_POOL + POOL_W
D_IN = OFF_GATE + N_BRANCH * D_MODEL

kernel_name = 'hybrid_mla_pool_dit_block'

def rms_norm(x, g):
    x32 = x.astype(jnp.float32)
    y = x32 * lax.rsqrt(jnp.mean(x32 * x32, axis=-1, keepdims=True) + EPS)
    return (y * g.astype(jnp.float32)).astype(x.dtype)

def modulate(h, shift, scale):
    return h * (1.0 + scale) + shift

def axial_angles(n_tokens):
    rows = n_tokens // GRID_W
    row = jnp.repeat(jnp.arange(rows), GRID_W)
    col = jnp.tile(jnp.arange(GRID_W), rows)
    pos = jnp.stack([row, col], axis=-1).astype(jnp.float32)
    inv_freq = ROPE_THETA ** (-jnp.arange(0, ROPE_AXIS, 2, dtype=jnp.float32) / ROPE_AXIS)
    return pos[:, :, None] * inv_freq

def apply_rope_2d(x, ang):
    shp = x.shape
    xr = x.astype(jnp.float32).reshape(shp[:-1] + (2, 2, QK_ROPE // 4))
    x1, x2 = xr[..., 0, :], xr[..., 1, :]
    cos, sin = jnp.cos(ang), jnp.sin(ang)
    out = jnp.stack([x1 * cos - x2 * sin, x1 * sin + x2 * cos], axis=-2)
    return out.reshape(shp).astype(x.dtype)

def mla_queries(z_q, q_norm, w_uq):
    q = rms_norm(z_q, q_norm) @ w_uq
    q = q.reshape(q.shape[:-1] + (N_HEADS, QK_NOPE + QK_ROPE))
    return q[..., :QK_NOPE], q[..., QK_NOPE:]

def mla_keys_values(z_kv, kv_norm, w_ukv):
    kv = rms_norm(z_kv, kv_norm) @ w_ukv
    kv = kv.reshape(kv.shape[:-1] + (N_HEADS, QK_NOPE + V_DIM))
    return kv[..., :QK_NOPE], kv[..., QK_NOPE:]

def attend(q_nope, q_rope, k_nope, k_rope, v):
    s = jnp.einsum('bqhd,bkhd->bhqk', q_nope, k_nope) + jnp.einsum('bqhr,bkr->bhqk', q_rope, k_rope)
    p = jax.nn.softmax(s.astype(jnp.float32) * ATTN_SCALE, axis=-1).astype(v.dtype)
    return jnp.einsum('bhqk,bkhd->bqhd', p, v)

def attend_blocked(q_nope, q_rope, k_nope, k_rope, v):
    b, t = q_nope.shape[:2]
    nb = t // Q_BLOCK
    qn = q_nope.reshape(b, nb, Q_BLOCK, N_HEADS, QK_NOPE).swapaxes(0, 1)
    qr = q_rope.reshape(b, nb, Q_BLOCK, N_HEADS, QK_ROPE).swapaxes(0, 1)
    o = lax.map(lambda qs: attend(qs[0], qs[1], k_nope, k_rope, v), (qn, qr))
    return o.swapaxes(0, 1).reshape(b, t, N_HEADS, V_DIM)

def multiscale_pool(u, w_pool, pool_scale, w_o_pool):
    b, t = u.shape[:2]
    cs = jnp.pad(jnp.cumsum(u.astype(jnp.float32), axis=1), ((0, 0), (1, 0), (0, 0)))
    pos = jnp.arange(t)
    groups = []
    for g, w in enumerate(POOL_WINDOWS):
        lo = jnp.clip(pos - w // 2, 0, t)
        hi = jnp.clip(pos + (w - w // 2), 0, t)
        sl = slice(g * POOL_GROUP, (g + 1) * POOL_GROUP)
        csg = cs[:, :, sl]
        mean = (csg[:, hi] - csg[:, lo]) / (hi - lo).astype(jnp.float32)[None, :, None]
        groups.append(mean.astype(u.dtype) - u[:, :, sl])
    d = jnp.stack(groups, axis=2)
    y = jnp.einsum('btgc,gce->btge', d, w_pool).reshape(b, t, POOL_W) * pool_scale
    return y @ w_o_pool

def mix_branches(z, o_att, w_o_mla, w_pool, pool_scale, w_o_pool, w_out):
    b, t = z.shape[:2]
    o_pool = multiscale_pool(z[..., OFF_POOL:OFF_GATE], w_pool, pool_scale, w_o_pool)
    gates = jax.nn.sigmoid(z[..., OFF_GATE:]).reshape(b, t, N_BRANCH, D_MODEL)
    merged = gates[:, :, 0] * (o_att.reshape(b, t, N_HEADS * V_DIM) @ w_o_mla) + gates[:, :, 1] * o_pool
    return merged @ w_out

def swiglu(h, w_gate, w_up, w_down):
    return (jax.nn.silu(h @ w_gate) * (h @ w_up)) @ w_down

def setup_inputs(seed: int = 0) -> dict:
    key = jax.random.key(seed)
    ks = jax.random.split(key, 24)
    f32 = jnp.float32

    def nrm(k, shape, fan_in):
        return jax.random.normal(k, shape, f32) * fan_in ** -0.5

    def gain(k, shape):
        return 1.0 + 0.05 * jax.random.normal(k, shape, f32)

    return {
        'x': jax.random.normal(ks[0], (BATCH, SEQ, D_MODEL), f32),
        'c': jax.random.normal(ks[1], (BATCH, D_MODEL), f32),
        'ctx': jax.random.normal(ks[2], (BATCH, CTX_LEN, D_MODEL), f32),
        'c_ctx': jax.random.normal(ks[3], (D_MODEL,), f32),
        'w_ada': nrm(ks[4], (DEPTH, D_MODEL, N_MOD * D_MODEL), D_MODEL),
        'b_ada': 0.01 * jax.random.normal(ks[5], (DEPTH, N_MOD * D_MODEL), f32),
        'g_pre_mix': gain(ks[6], (DEPTH, D_MODEL)),
        'w_in': nrm(ks[7], (DEPTH, D_MODEL, D_IN), D_MODEL),
        'q_norm': gain(ks[8], (DEPTH, Q_LORA)),
        'w_uq': nrm(ks[9], (DEPTH, Q_LORA, N_HEADS * (QK_NOPE + QK_ROPE)), Q_LORA),
        'kv_norm': gain(ks[10], (DEPTH, KV_LORA)),
        'w_ukv': nrm(ks[11], (DEPTH, KV_LORA, N_HEADS * (QK_NOPE + V_DIM)), KV_LORA),
        'w_o_mla': nrm(ks[12], (DEPTH, N_HEADS * V_DIM, D_MODEL), N_HEADS * V_DIM),
        'w_pool': nrm(ks[13], (DEPTH, N_POOL_GROUPS, POOL_GROUP, POOL_GROUP), POOL_GROUP),
        'pool_scale': 1.0 + 0.1 * jax.random.normal(ks[14], (DEPTH, POOL_W), f32),
        'w_o_pool': nrm(ks[15], (DEPTH, POOL_W, D_MODEL), POOL_W),
        'w_out': nrm(ks[16], (DEPTH, D_MODEL, D_MODEL), D_MODEL),
        'g_post_mix': gain(ks[17], (DEPTH, D_MODEL)),
        'g_pre_ffn': gain(ks[18], (DEPTH, D_MODEL)),
        'w_ffn_gate': nrm(ks[19], (DEPTH, D_MODEL, D_FF), D_MODEL),
        'w_ffn_up': nrm(ks[20], (DEPTH, D_MODEL, D_FF), D_MODEL),
        'w_ffn_down': nrm(ks[21], (DEPTH, D_FF, D_MODEL), D_FF),
        'g_post_ffn': gain(ks[22], (DEPTH, D_MODEL)),
    }

def reference(x, c, ctx, c_ctx, w_ada, b_ada, g_pre_mix, w_in, q_norm, w_uq, kv_norm, w_ukv, w_o_mla,
              w_pool, pool_scale, w_o_pool, w_out, g_post_mix, g_pre_ffn, w_ffn_gate, w_ffn_up, w_ffn_down,
              g_post_ffn):
    b, t, _ = x.shape
    ang = axial_angles(t).astype(x.dtype)
    xc = ctx
    for l in range(DEPTH):
        last = l == DEPTH - 1
        mod_x = (jax.nn.silu(c) @ w_ada[l] + b_ada[l]).reshape(b, 1, N_MOD, D_MODEL)
        mod_c = (jax.nn.silu(c_ctx) @ w_ada[l] + b_ada[l]).reshape(1, 1, N_MOD, D_MODEL)

        h = modulate(rms_norm(x, g_pre_mix[l]), mod_x[:, :, 1], mod_x[:, :, 0])
        hc = modulate(rms_norm(xc, g_pre_mix[l]), mod_c[:, :, 1], mod_c[:, :, 0])
        z = h @ w_in[l]
        if last:
            zc_kv = hc @ w_in[l][:, OFF_KV:OFF_POOL]
        else:
            zc = hc @ w_in[l]
            zc_kv = zc[..., OFF_KV:OFF_POOL]
        kc_nope, vc = mla_keys_values(zc_kv[..., :KV_LORA], kv_norm[l], w_ukv[l])
        kc_rope = zc_kv[..., KV_LORA:]
        q_nope, q_rope = mla_queries(z[..., :OFF_KV], q_norm[l], w_uq[l])
        q_rope = apply_rope_2d(q_rope, ang[:, None])
        k_nope, v = mla_keys_values(z[..., OFF_KV:OFF_KR], kv_norm[l], w_ukv[l])
        k_rope = apply_rope_2d(z[..., OFF_KR:OFF_POOL], ang)
        o = attend_blocked(q_nope, q_rope,
                           jnp.concatenate([kc_nope, k_nope], axis=1),
                           jnp.concatenate([kc_rope, k_rope], axis=1),
                           jnp.concatenate([vc, v], axis=1))
        y = mix_branches(z, o, w_o_mla[l], w_pool[l], pool_scale[l], w_o_pool[l], w_out[l])
        x = x + mod_x[:, :, 2] * rms_norm(y, g_post_mix[l])
        if not last:
            qc_nope, qc_rope = mla_queries(zc[..., :OFF_KV], q_norm[l], w_uq[l])
            oc = attend(qc_nope, qc_rope, kc_nope, kc_rope, vc)
            yc = mix_branches(zc, oc, w_o_mla[l], w_pool[l], pool_scale[l], w_o_pool[l], w_out[l])
            xc = xc + mod_c[:, :, 2] * rms_norm(yc, g_post_mix[l])

        hf = modulate(rms_norm(x, g_pre_ffn[l]), mod_x[:, :, 4], mod_x[:, :, 3])
        x = x + mod_x[:, :, 5] * rms_norm(swiglu(hf, w_ffn_gate[l], w_ffn_up[l], w_ffn_down[l]), g_post_ffn[l])
        if not last:
            hfc = modulate(rms_norm(xc, g_pre_ffn[l]), mod_c[:, :, 4], mod_c[:, :, 3])
            xc = xc + mod_c[:, :, 5] * rms_norm(swiglu(hfc, w_ffn_gate[l], w_ffn_up[l], w_ffn_down[l]), g_post_ffn[l])
    return x


_drawn_inputs = setup_inputs


def setup_inputs(seed=0):
    import zlib

    import numpy as np

    out = dict(_drawn_inputs(seed))
    spreads = {}
    factors = {'ctx': 2.71, 'b_ada': 2.88, 'q_norm': 8.0, 'kv_norm': 3.846}
    for name, (base, spread) in spreads.items():
        noise = np.random.default_rng([zlib.crc32(name.encode()), seed]).standard_normal(out[name].shape)
        drawn = base * np.exp(spread * noise) if base else spread * noise
        out[name] = __import__('jax').numpy.asarray(drawn.astype(out[name].dtype))
    for name, factor in factors.items():
        out[name] = (out[name] * factor).astype(out[name].dtype)
    return out
```

```python
from contextlib import ExitStack

import concourse.bass as bass
from concourse import mybir

P = 128
D_MODEL, SEQ, CTX, DEPTH = 1024, 512, 256, 2
HEADS, NOPE, ROPE, V_DIM = 8, 128, 64, 128
Q_LORA, KV_LORA, POOL_W, D_FF = 256, 128, 512, 2816
OFF_KV = Q_LORA
OFF_KR = OFF_KV + KV_LORA
OFF_POOL = OFF_KR + ROPE
OFF_GATE = OFF_POOL + POOL_W
GRID_W, THETA, EPS = 64, 10000.0, 1e-6
SCALE = float(NOPE + ROPE) ** -0.5

TOK = SEQ + CTX
DT = D_MODEL // P
KT_ALL = TOK // P
BLK = 2048
UNIT = 1024
WINDOWS = (2, 4, 8, 16)
NG = len(WINDOWS)
PAD = 8
U_LEN = PAD + SEQ + PAD + CTX + PAD
U_X, U_C = PAD, PAD + SEQ + PAD
FF_GROUPS = D_FF // 256
PAIRS = HEADS // 2

VEC_ROWS = (("b_ada", 48), ("g_pre_mix", 8), ("g_post_mix", 8), ("g_pre_ffn", 8), ("g_post_ffn", 8),
            ("q_norm", 2), ("kv_norm", 1), ("pool_scale", 4), ("c", 8), ("c_ctx", 8))


def vec_columns():
    at, out = 0, {}
    for name, n in VEC_ROWS:
        out[name] = (at, at + n)
        at += n
    return out, at


class Phase:

    def __init__(self, plan, blocks, reads, turns):
        self.b, self.g, self.ra, self.rd = plan.b, plan.g, plan.ra, plan.rd
        self.blocks, self.groups, self.turns = blocks, len(reads), turns
        self.read = []
        a = d = 0
        for r in reads:
            if r == "A":
                a += 1
            if r == "D":
                d += 1
            self.read.append(("A", plan.ra + a + (r == "a")) if r in "Aa" else ("D", plan.rd + d + (r == "d")))
        self.da, self.dd = a, d
        plan.b += blocks * turns
        plan.g += len(reads) * turns
        plan.ra += a * turns
        plan.rd += d * turns


class Plan:

    def __init__(self):
        self.b = self.g = self.ra = self.rd = 0
        self.ph = {}
        self.end = {}
        self.norms = {}
        self.adds = self.nk_all = self.upd = self.lo_all = self.full = self.n_norm = 0

        def add(key, blocks, reads, turns=1, ends=()):
            p = self.ph[key] = Phase(self, blocks, reads, turns)
            for t in range(turns):
                for j, e in enumerate(ends):
                    self.end[p.b + t * blocks + j] = p.g + t * len(reads) + e

        def norm(key, nk, tokens, post=False):
            self.norms[key] = dict(nk=nk, T=tokens, adds=self.adds, sq=self.nk_all, rest=self.lo_all, full=self.full,
                                   upd=self.upd, n=self.n_norm)
            self.adds += nk - 1
            self.nk_all += nk
            self.n_norm += 1
            if post:
                self.upd += nk - 1
            else:
                self.lo_all += nk - 1
                self.full += nk
            add(key, 0, "DD")

        add("vectors", 0, "D" * DEPTH)
        add("x_in", 0, "A" * DT)
        for l in range(DEPTH):
            T = TOK if l == 0 else SEQ
            add(("ada", l), 2, "AADD", 4, (1, 2))
            norm(("pre_mix", l), DT, TOK)
            add(("u", l), 2, "AAAA", 1, (2, 4))
            add(("qkv", l), 3, "AAADD", 1, (2, 3, 5))
            add(("g0", l), 2, "AAAA", 2, (2, 4))
            norm(("q", l), 2, T)
            norm(("kv", l), 1, TOK)
            add(("g1", l), 2, "AAAA", 2, (2, 4))
            add(("w_pool", l), 1, "DDDD", 1, (4,))
            add(("w_o_pool", l), 2, "D" * 8, 1, (4, 8))
            nv = 4 if l == 0 else 2
            seq = attention_order(l)
            kinds = "".join("A" if k == "S" else "D" for k, _ in seq)
            reads = "DD" + "DD" + "DD" + "D" * nv + "AADD" + kinds + "AADD" + "D" * 8
            n0 = 6 + nv
            end_att = n0 + 4 + len(seq)
            add(("pairs", l), 6, reads, PAIRS,
                (n0, n0 + 1, n0 + 2, end_att + 1, end_att + 2, end_att + 4 + 8))
            add(("w_out", l), 2, "AAAA", 2, (2, 4))
            norm(("post_mix", l), DT, T, True)
            norm(("pre_ffn", l), DT, T)
            add(("ff_first", l), 2, "dDdD", 1, (2, 4))
            add(("ff", l), 6, ("dDdD" + "D" * 8) * 2, (FF_GROUPS - 1) // 2, (2, 4, 12, 14, 16, 24))
            add(("ff_last", l), 1, "D" * 8, 1, (8,))
            norm(("post_ffn", l), DT, T, True)
        add("out", 0, "A" * (SEQ // P))


def attention_tiles(l):
    out = []
    for h in range(2):
        out += [(h, n, False) for n in range(SEQ // P)]
        if l == 0:
            out.append((h, 0, True))
    return out


def pv_sets(l):
    out, now = {}, []
    for t, (h, n, c) in enumerate(attention_tiles(l)):
        now.append(t)
        if c or len(now) == 2:
            out[t] = (len(out), tuple(now))
            now = []
    return out


def attention_order(l):
    n, sets, waiting, out = len(attention_tiles(l)), pv_sets(l), [], [("S", 0), ("S", 1)]
    for t in range(n):
        out.append(("T", t))
        if t + 2 < n:
            out.append(("S", t + 2))
        if waiting:
            out.append(("V", waiting.pop()))
        if t in sets:
            waiting.append(sets[t][0])
    out.append(("V", waiting.pop()))
    return out


def backbone_kernel(nc, x, c, ctx, c_ctx, w_ada, b_ada, g_pre_mix, w_in, q_norm, w_uq, kv_norm, w_ukv, w_o_mla,
                    w_pool, pool_scale, w_o_pool, w_out, g_post_mix, g_pre_ffn, w_ffn_gate, w_ffn_up,
                    w_ffn_down, g_post_ffn, k_ident, k_rope, k_edge, k_pair, out, x_keep):
    f32, f32r = mybir.dt.float32, mybir.dt.float32r
    ACT, ALU, AX = mybir.ActivationFunctionType, mybir.AluOpType, mybir.AxisListType
    ds = bass.ds
    plan = Plan()
    ph = plan.ph
    vec, n_vec = vec_columns()
    es = ExitStack()
    with es:
        def sb(name, shape, dt=f32):
            return es.enter_context(nc.sbuf_tensor(name, shape, dt))

        def sem(name):
            return es.enter_context(nc.semaphore(name))

        stage = sb("stage", [P, 2, BLK])
        w_hi = sb("w_hi", [P, 2, BLK], f32r)
        w_lo = sb("w_lo", [P, 2, BLK], f32r)
        HT, QT = DT * TOK, 6 * TOK
        arena = sb("arena", [P, 26112], f32r)

        def part(at, n, width):
            return arena[:, at:at + n * width].rearrange("p (n t) -> p n t", n=n)
        at = 0
        ql = [part(at + i * 2 * TOK, 2, TOK) for i in range(2)]
        at += 4 * TOK
        kvl = [part(at + i * TOK, 1, TOK) for i in range(2)]
        at += 2 * TOK
        kr = [part(at + i * TOK, 1, TOK) for i in range(2)]
        at += 2 * TOK
        base = at
        h = [part(base + i * HT, DT, TOK) for i in range(2)]
        pd = [part(base + 2 * HT + i * 4 * TOK, 4, TOK) for i in range(2)]
        hid = [[part(base + 2 * HT + (2 * s + i) * 2 * TOK, 2, TOK) for i in range(2)] for s in range(2)]
        mg = h
        at = base
        qn = [part(at + i * 2 * TOK, 2, TOK) for i in range(2)]
        at += 4 * TOK
        qr = [part(at + i * TOK, 1, TOK) for i in range(2)]
        at += 2 * TOK
        kn = [part(at + i * 2 * TOK, 2, TOK) for i in range(2)]
        at += 4 * TOK
        vv = [part(at + i * KT_ALL * 256, KT_ALL, 256) for i in range(2)]
        at += 2 * KT_ALL * 256
        pt = [[part(at + (2 * s + i) * KT_ALL * 256, KT_ALL, 256) for i in range(2)] for s in range(2)]
        at += 4 * KT_ALL * 256
        oo = [part(at + i * 2 * TOK, 2, TOK) for i in range(2)]
        at += 4 * TOK
        assert at <= 26112
        cst = sb("cst", [P, DT * 4 + 124], f32r)
        big = sb("big", [P, 2 * DT, TOK])
        xs, ys = big[:, 0:DT, :], big[:, DT:2 * DT, :]
        ybuf = ys.rearrange("p n t -> p (n t)")
        u_pad = ybuf[:, 0:NG * U_LEN].rearrange("p (g t) -> p g t", g=NG)
        raw = ybuf[:, NG * U_LEN:NG * U_LEN + 3 * TOK].rearrange("p (n t) -> p n t", n=3)
        tmp_all = sb("tmp", [P, 2 * U_LEN + 3 * TOK])
        tmp = [tmp_all[:, i * U_LEN:i * U_LEN + TOK] for i in range(2)]
        tmp += [tmp_all[:, 2 * U_LEN + i * TOK:2 * U_LEN + (i + 1) * TOK] for i in range(3)]
        ptmp = [tmp_all[:, i * U_LEN:(i + 1) * U_LEN] for i in range(2)]
        rope_t = sb("rope_t", [P, 2, SEQ])
        ident = sb("ident", [P, P])
        ones = sb("ones", [P, P])
        edge = sb("edge", [P, NG, 2, 2, PAD])
        pair_sum = sb("pair_sum", [4, 2])
        vecs = sb("vecs", [P, DEPTH, n_vec])
        mods = sb("mods", [P, 48, 2])
        gain = sb("gain", [P, 4, DT, 2])
        csil = sb("csil", [P, 16])
        mrow = sb("mrow", [4, 2, 256])
        small = sb("small", [P, 16])
        msq, rstd = small[:, 0:6], small[:, 8:14]
        zero = sb("zero", [P, 1])
        power = sb("power", [P, TOK // P])
        st = sb("st", [P, 2, 8])
        acc = es.enter_context(nc.psum_tensor("acc", [P, 4 * UNIT], f32))

        def unit(g):
            return acc[:, (g % 4) * UNIT:(g % 4 + 1) * UNIT]

        stage_full = [sem("stage_full0"), sem("stage_full1")]
        whi_ready, wlo_ready = sem("whi_ready"), sem("wlo_ready")
        mm_done, read_a, read_d = sem("mm_done"), sem("read_a"), sem("read_d")
        ident_in, consts_in, x_in, rows_in = sem("ident_in"), sem("consts_in"), sem("x_in"), sem("rows_in")
        cleared, x_saved, x_back, out_sent = sem("cleared"), sem("x_saved"), sem("x_back"), sem("out_sent")
        c_ready, mods_step = sem("c_ready"), sem("mods_step")
        sq_done, sq_added, rstd_done, diag_done = sem("sq_done"), sem("sq_added"), sem("rstd_done"), sem("diag_done")
        n_scaled, n_hi, n_full, n_lo, x_upd = sem("n_scaled"), sem("n_hi"), sem("n_full"), sem("n_lo"), sem("x_upd")
        pool_step, pool_done, pd_hi, pd_lo = sem("pool_step"), sem("pool_done"), sem("pd_hi"), sem("pd_lo")
        wp_hi, swap_hi, swap_lo = sem("wp_hi"), sem("swap_hi"), sem("swap_lo")
        rope_sum, rope_step, rope_hi, rope_lo = sem("rope_sum"), sem("rope_step"), sem("rope_hi"), sem("rope_lo")
        proj_hi, smax, p_norm, pt_hi, o_hi = sem("proj_hi"), sem("smax"), sem("p_norm"), sem("pt_hi"), sem("o_hi")
        merged_add, mg_hi, mg_lo = sem("merged_add"), sem("mg_hi"), sem("mg_lo")
        silu_done, hid_hi, hid_lo, y_clear = sem("silu_done"), sem("hid_hi"), sem("hid_lo"), sem("y_clear")

        rows = ybuf.rearrange("p (t n) -> p t n", t=KT_ALL)
        vrow = [tmp[0][:, 0:P], tmp[1][:, 0:P]]

        def tokens(l):
            return TOK if l == 0 else SEQ

        def segs(n):
            return [(0, SEQ)] + ([(SEQ, n)] if n > SEQ else [])

        def freed(p, j, i):
            e, n = p.read[j - 4] if j >= 4 else p.read[j - 4 + p.groups]
            step = p.da if e == "A" else p.dd
            if j < 4:
                n -= step
            return (read_a if e == "A" else read_d), n + i * step

        def two(dst, src, n):
            a = n // 2
            return [(dst[:, 0:a], src[:, 0:a]), (dst[:, a:n], src[:, a:n])]

        def as3(slot, n, w):
            return stage[:, slot, 0:n * w].rearrange("p (n w) -> p n w", n=n)

        def k_major(w, l):
            return w[l].rearrange("(k p) n -> p k n", p=P)

        def load(kind, l, j, slot):
            if kind == "ada":
                return two(as3(slot, DT, 256), k_major(w_ada, l)[:, :, ds(j * 256, 256)], DT)
            if kind == "in":
                return two(as3(slot, DT, 256), k_major(w_in, l)[:, :, ds(j, 256)], DT)
            if kind == "kv":
                return two(as3(slot, DT, 128), k_major(w_in, l)[:, :, ds(OFF_KV, 128)], DT)
            if kind == "kr":
                src = k_major(w_in, l)[:, :, ds(OFF_KR, ROPE)]
                dst = as3(slot, DT, 256)
                return [(dst[:, :, 0:ROPE], src), (dst[:, :, ROPE:2 * ROPE], src)]
            if kind == "pool":
                return two(as3(slot, NG, P), w_pool[l].rearrange("g c e -> c g e"), NG)
            if kind == "o_pool":
                return two(as3(slot, 4, 512), k_major(w_o_pool, l)[:, :, ds(j * 512, 512)], 4)
            if kind == "qk":
                return [(as3(slot, 2, 384), k_major(w_uq, l)[:, :, ds(j * 384, 384)]),
                        (stage[:, slot, 768:1280], w_ukv[l][:, ds(j * 512, 512)])]
            if kind == "o":
                return two(as3(slot, 2, D_MODEL), w_o_mla[l][ds(j * 256, 256), :].rearrange("(k p) n -> p k n", p=P), 2)
            if kind == "out":
                return two(as3(slot, DT, 256), k_major(w_out, l)[:, :, ds(j * 256, 256)], DT)
            if kind == "gate":
                return two(as3(slot, DT, 256), k_major(w_ffn_gate, l)[:, :, ds(j * 256, 256)], DT)
            if kind == "up":
                return two(as3(slot, DT, 256), k_major(w_ffn_up, l)[:, :, ds(j * 256, 256)], DT)
            return two(as3(slot, 2, D_MODEL),
                       w_ffn_down[l][ds(j * 256, 256), :].rearrange("(k p) n -> p k n", p=P), 2)

        block = es.enter_context(nc.Block())

        @block.sync
        def _(sp):
            sp.dma_start(ident[:], k_ident).then_inc(ident_in, 16)
            for l in range(DEPTH):
                own = {"b_ada": b_ada, "g_pre_mix": g_pre_mix, "g_post_mix": g_post_mix, "g_pre_ffn": g_pre_ffn,
                       "g_post_ffn": g_post_ffn, "q_norm": q_norm, "kv_norm": kv_norm, "pool_scale": pool_scale}
                for name, (a, b) in vec.items():
                    src = c[0] if name == "c" else c_ctx if name == "c_ctx" else own[name][l]
                    sp.dma_start(vrow[l][a:b, :], src.rearrange("(r q) -> r q", q=P)).then_inc(rows_in, 16)

            def put(kind, l, j, b, p=None, i=0):
                step = p.blocks if p else 0
                if b >= 2:
                    sp.wait_ge(wlo_ready, b - 1 + i * step)
                for dst, src in load(kind, l, j, b % 2):
                    sp.dma_start(dst, src).then_inc(stage_full[b % 2], 16)

            for l in range(DEPTH):
                p = ph["ada", l]
                if l == 0:
                    put("ada", 0, 0, p.b)
                    put("ada", 0, 1, p.b + 1)
                    for t in range(TOK // P):
                        src = x[0, t * P:(t + 1) * P, :] if t < SEQ // P else ctx[0, t * P - SEQ:(t + 1) * P - SEQ, :]
                        sp.dma_start(rows[:, t, :], src).then_inc(x_in, 16)
                    sp.dma_start(rope_t[:], k_rope).then_inc(consts_in, 16)
                    sp.dma_start(edge[:], k_edge).then_inc(consts_in, 16)
                    sp.dma_start(pair_sum[:], k_pair).then_inc(consts_in, 16)
                sent = 1 if l == 0 else 0
                with sp.Fori(0, p.turns - sent) as i:
                    for s in range(2):
                        put("ada", l, 2 * i + (2 * sent + s), p.b + 2 * sent + s, p, i)
                p = ph["u", l]
                put("in", l, OFF_POOL, p.b)
                put("in", l, OFF_POOL + 256, p.b + 1)
                p = ph["qkv", l]
                put("in", l, 0, p.b)
                put("kv", l, 0, p.b + 1)
                put("kr", l, 0, p.b + 2)
                for half in range(2):
                    p = ph["g%d" % half, l]
                    with sp.Fori(0, p.turns) as i:
                        for s in range(2):
                            put("in", l, (2 * i + s) * 256 + OFF_GATE + half * D_MODEL, p.b + s, p, i)
                put("pool", l, 0, ph["w_pool", l].b)
                for s in range(2):
                    put("o_pool", l, s, ph["w_o_pool", l].b + s)
                p = ph["pairs", l]
                with sp.Fori(0, p.turns) as i:
                    put("qk", l, i, p.b, p, i)
                    for s in range(4):
                        put("ada", l, 4 * i + (8 + s), p.b + 1 + s, p, i)
                    put("o", l, i, p.b + 5, p, i)
                p = ph["w_out", l]
                with sp.Fori(0, p.turns) as i:
                    for s in range(2):
                        put("out", l, 2 * i + s, p.b + s, p, i)
                p = ph["ff_first", l]
                put("gate", l, 0, p.b)
                put("up", l, 0, p.b + 1)
                p = ph["ff", l]
                with sp.Fori(0, p.turns) as i:
                    for s in range(2):
                        put("gate", l, 2 * i + (s + 1), p.b + 3 * s, p, i)
                        put("up", l, 2 * i + (s + 1), p.b + 3 * s + 1, p, i)
                        put("down", l, 2 * i + s, p.b + 3 * s + 2, p, i)
                put("down", l, FF_GROUPS - 1, ph["ff_last", l].b)
            p = ph["out"]
            for t in range(SEQ // P):
                sp.wait_ge(read_a, p.read[t][1])
                sp.dma_start(out[0, t * P:(t + 1) * P, :], rows[:, t, :]).then_inc(out_sent, 16)
            sp.wait_ge(out_sent, 16 * (SEQ // P))

        def after(per_pair, l, i, k):
            return l * PAIRS * per_pair[0] + i * per_pair[l] + k

        N_TILES = [len(attention_tiles(l)) for l in range(DEPTH)]
        N_STAT = [2 * n for n in N_TILES]
        N_PV = [len(pv_sets(l)) for l in range(DEPTH)]
        V_TILES = [[(0, 2), (2, 4), (4, 5), (5, 6)], [(0, 4), (4, 6)]]
        N_PROJ = [4 + len(v) for v in V_TILES]

        def as_values(u, n):
            return u[:, 0:n * 256].rearrange("p (n w) -> p n w", n=n)

        def score_places(l, t, u):
            e = tmp[3 + t % 2]
            if attention_tiles(l)[t][2]:
                return [(u[:, 0:CTX], e[:, 0:CTX]), (u[:, SEQ:SEQ + CTX], e[:, CTX:2 * CTX])]
            return [(u[:, 0:TOK], e[:, 0:TOK])]

        def turned_places(l, t, u):
            _, n, of_ctx = attention_tiles(l)[t]
            k = next(k for k, own in pv_sets(l).values() if t in own)
            if of_ctx:
                return u[:, 0:2 * CTX].rearrange("p (n w) -> p n w", n=2), [pt[k % 2][i][:, 0:2, :] for i in range(2)]
            a = (n % 2) * P
            return (u[:, 0:TOK].rearrange("p (n w) -> p n w", n=KT_ALL),
                    [pt[k % 2][i][:, :, a:a + P] for i in range(2)])

        def pv_place(l, k):
            own = next(own for n, own in pv_sets(l).values() if n == k)
            hd, n, of_ctx = attention_tiles(l)[own[-1]]
            return (hd, SEQ, SEQ // P) if of_ctx else (hd, (n // 2) * 256, 0)

        def swap_places(w, keys, half):
            if keys:
                v = w.rearrange("p (k s a h c) -> p k s a h c", k=DT, s=2, a=4, h=2)
                return v[:, :, 0, :, half, :], v[:, :, 1, :, 1 - half, :]
            q = w[:, 0:768].rearrange("p (k n) -> p k n", k=4)[:, :, NOPE:NOPE + ROPE]
            src = q.rearrange("p k (a h c) -> p k a h c", a=2, h=2)
            dst = w[:, 1536:1792].rearrange("p (k a h c) -> p k a h c", k=4, a=2, h=2)
            return src[:, :, :, half, :], dst[:, :, :, 1 - half, :]

        def rope_places(w):
            return (w[:, 0:768].rearrange("p (k n) -> p k n", k=4)[:, :, NOPE:NOPE + ROPE],
                    w[:, 1280:1536].rearrange("p (k n) -> p k n", k=4))

        def updated(e, key, k):
            n = plan.norms[key]
            if k < n["nk"] - 1:
                e.wait_ge(x_upd, n["upd"] + k + 1)
            else:
                e.wait_ge(read_d, ph[key].read[1][1])

        def x_ready(e, key, k):
            what, l = key
            if what == "pre_ffn":
                updated(e, ("post_mix", l), k)
            elif l:
                updated(e, ("post_ffn", l - 1), k)
            else:
                e.wait_ge(read_a, ph["x_in"].read[k][1])

        def scale_of(key, k, v):
            what, l = key
            if what == "q":
                return vecs[:, l, vec["q_norm"][0] + k:vec["q_norm"][0] + k + 1]
            if what == "kv":
                return vecs[:, l, vec["kv_norm"][0]:vec["kv_norm"][0] + 1]
            n = {"pre_mix": 0, "post_mix": 1, "pre_ffn": 2, "post_ffn": 3}[what]
            return gain[:, n, k, v:v + 1]

        def shift_of(key, k, v):
            if key[0] in ("q", "kv"):
                return zero[:]
            m = {"pre_mix": DT, "pre_ffn": 4 * DT}[key[0]]
            return mods[:, m + k, v:v + 1]

        def steps_of_pool(l, g):
            streams = 2 if l == 0 else 1
            per = [n + 1 + 2 * streams + 2 for n in range(NG)]
            before = 0 if l == 0 else 3 + sum(n + 1 + 4 + 2 for n in range(NG))
            return before + 3 + sum(per[:g + 1])

        @block.gpsimd
        def _(pool):
            nc.gpsimd.memset(ones[:], 1.0).then_inc(cleared, 1)
            nc.gpsimd.memset(zero[:], 0.0).then_inc(cleared, 1)
            nc.gpsimd.memset(cst[:].bitcast(f32), 0.0).then_inc(cleared, 1)
            nc.gpsimd.memset(power[:], -0.5).then_inc(cleared, 1)
            pool.wait_ge(cleared, 4)

            def norm(key):
                n, T = plan.norms[key], plan.norms[key]["T"]
                pool.wait_ge(read_d, ph[key].read[0][1])
                nc.gpsimd.tensor_tensor(rstd[:, 0:T // P], msq[:, 0:T // P], power[:, 0:T // P], ALU.pow
                                        ).then_inc(rstd_done, 1)
                if key[0].startswith("post"):
                    return
                for k in range(n["nk"]):
                    pool.wait_ge(n_scaled, n["sq"] + k + 1)
                    for v, (a, b) in enumerate(segs(T)):
                        last = nc.gpsimd.tensor_scalar(tmp[3 + k % 2][:, a:b], tmp[k % 2][:, a:b],
                                                       scale_of(key, k, v), shift_of(key, k, v), ALU.mult, ALU.add)
                    last.then_inc(n_full, 1)

            for l in range(DEPTH):
                norm(("pre_mix", l))
                n = (l > 0) * steps_of_pool(0, NG - 1)
                for a, b in ((0, U_X), (U_X + SEQ, U_C), (U_C + CTX, U_LEN)):
                    nc.gpsimd.memset(u_pad[:, :, a:b], 0.0).then_inc(pool_step, 1)
                n += 3
                pool.wait_ge(read_a, ph["u", l].read[-1][1])
                a, b = U_X, (U_C + CTX if l == 0 else U_X + SEQ)
                for g, w in enumerate(WINDOWS):
                    src, m = u_pad[:, g, :], 1
                    for level in range(g + 1):
                        dst, cols = ptmp[level % 2], b + PAD - 2 * m + 1
                        pool.wait_ge(pool_step, n)
                        nc.gpsimd.tensor_tensor(dst[:, 0:cols], src[:, 0:cols], src[:, m:m + cols], ALU.add
                                                ).then_inc(pool_step, 1)
                        src, m, n = dst, 2 * m, n + 1
                    half = w // 2
                    for side, at in ((0, U_X), (1, U_X + SEQ - PAD)):
                        for t in range(2 if l == 0 else 1):
                            at_t = at + t * (U_C - U_X if side == 0 else U_C + CTX - U_X - SEQ) - half
                            pool.wait_ge(pool_step, n)
                            nc.gpsimd.tensor_tensor(src[:, at_t:at_t + PAD], src[:, at_t:at_t + PAD],
                                                    edge[:, g, side, t, :], ALU.mult).then_inc(pool_step, 1)
                            n += 1
                    pool.wait_ge(pool_step, n)
                    nc.gpsimd.tensor_scalar(src[:, a - half:b - half], src[:, a - half:b - half], 1.0 / w, 0.0,
                                            ALU.mult, ALU.add).then_inc(pool_step, 1)
                    pool.wait_ge(pool_step, n + 1)
                    nc.gpsimd.tensor_tensor(u_pad[:, g, a:b], src[:, a - half:b - half], u_pad[:, g, a:b],
                                            ALU.subtract).then_inc(pool_step, 1)
                    n += 2
                    assert n == steps_of_pool(l, g)
                for key in (("q", l), ("kv", l), ("post_mix", l), ("pre_ffn", l)):
                    norm(key)
                nc.gpsimd.memset(ys, 0.0).then_inc(y_clear, 1)
                norm(("post_ffn", l))

        @block.scalar
        def _(act):
            def split(b, p, i=0):
                act.wait_ge(stage_full[b % 2], 32 * (b // 2 + 1) + i * (16 * p.blocks))
                if b >= 2:
                    act.wait_ge(mm_done, (p.g if b - 2 < p.b else plan.end[b - 2]) + i * p.groups)
                nc.scalar.activation(w_hi[:, b % 2, :], stage[:, b % 2, :], ACT.Copy).then_inc(whi_ready, 1)

            def copy_out(p, j, dst, n, i=0, func=ACT.Copy):
                act.wait_ge(mm_done, p.g + j + 1 + i * p.groups)
                nc.scalar.activation(dst, unit(p.g + j)[:, 0:n], func).then_inc(read_a, 1)

            def swap(b, p, keys, i=0):
                act.wait_ge(wlo_ready, b + 1 + i * p.blocks)
                if not keys:
                    nc.scalar.activation(rope_places(w_hi[:, b % 2, :])[1],
                                         rope_places(w_hi[:, b % 2, :].bitcast(f32))[0], ACT.Copy)
                for half in range(2):
                    src, _ = swap_places(w_hi[:, b % 2, :].bitcast(f32), keys, half)
                    _, dst = swap_places(w_hi[:, b % 2, :], keys, half)
                    last = nc.scalar.activation(dst, src, ACT.Copy) if half == 0 else \
                        nc.scalar.activation(dst, src, ACT.Copy).then_inc(swap_hi, 1)

            def squares(key, src, ready):
                n = plan.norms[key]
                if n["full"]:
                    act.wait_ge(n_full, n["full"])
                    act.wait_ge(n_hi, n["full"])
                for k in range(n["nk"]):
                    ready(k)
                    if k >= 2:
                        act.wait_ge(sq_added, n["adds"] + max(k - 2, 1))
                    nc.scalar.activation(tmp[k % 2][:, 0:n["T"]], src[:, k, 0:n["T"]], ACT.Square
                                         ).then_inc(sq_done, 1)

            def norm_hi(key, hi):
                n = plan.norms[key]
                for k in range(n["nk"]):
                    act.wait_ge(n_scaled, n["sq"] + k + 1)
                    for v, (a, b) in enumerate(segs(n["T"])):
                        last = nc.scalar.activation(hi[:, k, a:b], tmp[k % 2][:, a:b], ACT.Identity,
                                                    bias=shift_of(key, k, v), scale=scale_of(key, k, v))
                    last.then_inc(n_hi, 1)

            def ada_rows(p, b, j, i):
                for s in range(2):
                    split(b + s + 1, p, i)
                    act.wait_ge(mm_done, p.g + j + s + 1 + i * p.groups)
                    nc.scalar.activation(mrow[:, s, :], unit(p.g + j + s)[0:4, 0:256], ACT.Copy).then_inc(read_a, 1)

            split(0, ph["ada", 0])
            act.wait_ge(read_d, ph["vectors"].read[0][1])
            a = vec["c"][0]
            nc.scalar.activation(csil[:], vecs[:, 0, a:a + 2 * DT], ACT.Silu).then_inc(c_ready, 1)
            act.wait_ge(c_ready, 1)
            act.wait_ge(cleared, 4)
            for v in range(2):
                nc.scalar.activation(cst[:, 0:DT * 4].rearrange("p (k f) -> p k f", f=4)[:, :, 2 * v],
                                     csil[:, v * DT:(v + 1) * DT], ACT.Copy).then_inc(c_ready, 1)
            for k in range(DT):
                copy_out(ph["x_in"], k, xs[:, k, :], TOK)
            for l in range(DEPTH):
                T = tokens(l)
                p = ph["ada", l]
                with act.Fori(0, p.turns) as i:
                    ada_rows(p, p.b, 0, i)
                key = ("pre_mix", l)
                squares(key, xs, lambda k: x_ready(act, key, k))
                act.dma_start(x_keep[:, :, 0:T], xs[:, :, 0:T]).then_inc(x_saved, 16)
                norm_hi(key, h[0])
                p = ph["u", l]
                for s in range(2):
                    split(p.b + s + 1, p)
                    for j in (2 * s, 2 * s + 1):
                        act.wait_ge(mm_done, p.g + j + 1)
                        if l == 0:
                            nc.scalar.activation(u_pad[:, j, U_C:U_C + CTX], unit(p.g + j)[:, SEQ:TOK], ACT.Copy)
                        nc.scalar.activation(u_pad[:, j, U_X:U_X + SEQ], unit(p.g + j)[:, 0:SEQ], ACT.Copy
                                             ).then_inc(read_a, 1)
                p = ph["qkv", l]
                split(p.b + 1, p)
                copy_out(p, 0, raw[:, 0, 0:T], T)
                copy_out(p, 1, raw[:, 1, 0:T], T)
                split(p.b + 2, p)
                copy_out(p, 2, raw[:, 2, :], TOK)
                swap(p.b + 2, p, True)
                split(p.b + 3, p)
                act.wait_ge(rope_sum, 1 + l * (PAIRS + 1))
                nc.scalar.activation(kr[0][:, 0, :], tmp[2][:, :], ACT.Copy).then_inc(rope_hi, 1)
                for half in range(2):
                    p = ph["g%d" % half, l]
                    if half == 0:
                        act.wait_ge(x_saved, 16 * (l + 1))
                    else:
                        for g in range(NG):
                            act.wait_ge(pool_step, steps_of_pool(l, g))
                            for v, (a, b) in enumerate(segs(T)):
                                off = U_C - SEQ if v else U_X
                                last = nc.scalar.activation(pd[0][:, g, a:b], u_pad[:, g, a + off:b + off], ACT.Copy)
                            last.then_inc(pd_hi, 1)
                        for what, src, dst in (("q", raw[:, 0:2, :], ql), ("kv", raw[:, 2:3, :], kvl)):
                            squares((what, l), src, lambda k: None)
                            norm_hi((what, l), dst[0])
                        act.wait_ge(pd_lo, NG * (l + 1))
                    with act.Fori(0, p.turns) as i:
                        for s in range(2):
                            split(p.b + s + 1, p, i)
                            for j in (2 * s, 2 * s + 1):
                                copy_out(p, j, big[:, ds(4 * i + (half * DT + j), 1), 0:T], T, i, ACT.Sigmoid)
                p = ph["w_pool", l]
                split(p.b + 1, p)
                a = vec["pool_scale"][0]
                for g in range(NG):
                    act.wait_ge(mm_done, p.g + g + 1)
                    nc.scalar.activation(pd[0][:, g, 0:T], unit(p.g + g)[:, 0:T], ACT.Copy,
                                         scale=vecs[:, l, a + g:a + g + 1]).then_inc(wp_hi, 1)
                p = ph["w_o_pool", l]
                split(p.b + 1, p)
                split(p.b + 2, p)
                p = ph["pairs", l]
                with act.Fori(0, p.turns) as i:
                    def parts(j, dst, src):
                        act.wait_ge(mm_done, p.g + j + 1 + i * p.groups)
                        nc.scalar.activation(dst, src, ACT.Copy).then_inc(proj_hi, 1)
                    swap(p.b, p, False, i)
                    split(p.b + 1, p, i)
                    for hd in range(2):
                        parts(hd, qn[0][:, hd, 0:T], unit(p.g + hd)[:, 0:T])
                    act.wait_ge(rope_sum, 2 + l * (PAIRS + 1) + i)
                    nc.scalar.activation(qr[0][:, 0, 0:T], tmp[2][:, 0:T], ACT.Copy).then_inc(rope_hi, 1)
                    for hd in range(2):
                        parts(4 + hd, kn[0][:, hd, :], unit(p.g + 4 + hd)[:, 0:TOK])
                    for j, (a, b) in enumerate(V_TILES[l]):
                        parts(6 + j, vv[0][:, a:b, :], as_values(unit(p.g + 6 + j), b - a))
                    j0 = 6 + len(V_TILES[l])
                    ada_rows(p, p.b + 1, j0, i)
                    j0 += 4
                    for n, (kind, t) in enumerate(attention_order(l)):
                        u = unit(p.g + j0 + n)
                        act.wait_ge(mm_done, p.g + j0 + n + 1 + i * p.groups)
                        if kind == "S":
                            act.wait_ge(smax, after(N_STAT, l, i, 2 * t + 2))
                            for v, (src, dst) in enumerate(score_places(l, t, u)):
                                last = nc.scalar.activation(dst, src, ACT.Exp, bias=st[:, t % 2, 2 + v:3 + v],
                                                            scale=SCALE, accum_out=st[:, t % 2, 4 + v:5 + v])
                            last.then_inc(read_a, 1)
                        elif kind == "T":
                            src, dst = turned_places(l, t, u)
                            nc.scalar.activation(dst[0], src, ACT.Copy).then_inc(pt_hi, 1)
                        else:
                            hd, a, _ = pv_place(l, t)
                            nc.scalar.activation(oo[0][:, hd, a:a + 256], u[:, 0:256], ACT.Copy).then_inc(o_hi, 1)
                    ada_rows(p, p.b + 3, j0 + len(attention_order(l)), i)
                    split(p.b + 6, p, i)
                for k in range(DT):
                    act.wait_ge(merged_add, (l + 1) * PAIRS * DT - DT + k + 1)
                    nc.scalar.activation(mg[0][:, k, 0:T], ys[:, k, 0:T], ACT.Copy).then_inc(mg_hi, 1)
                act.dma_start(xs[:, :, 0:T], x_keep[:, :, 0:T]).then_inc(x_back, 16)
                act.wait_ge(mg_lo, (l + 1) * DT)
                p = ph["w_out", l]
                with act.Fori(0, p.turns) as i:
                    for s in range(2):
                        split(p.b + s + 1, p, i)
                        for j in (2 * s, 2 * s + 1):
                            copy_out(p, j, ys[:, ds(4 * i + j, 1), 0:T], T, i)
                p = ph["w_out", l]
                squares(("post_mix", l), ys, lambda k: act.wait_ge(read_a, p.ra + k + 1))
                squares(("pre_ffn", l), xs, lambda k: x_ready(act, ("pre_ffn", l), k))
                norm_hi(("pre_ffn", l), h[0])

                def hidden(p, j, n, i=0):
                    for m in range(2):
                        act.wait_ge(mm_done, p.g + j + m + 1 + i * p.groups)
                        nc.scalar.activation(tmp[m][:, 0:T], unit(p.g + j + m)[:, 0:T], ACT.Silu
                                             ).then_inc(silu_done, 1)

                def hidden_hi(p, j, s, i=0):
                    for m in range(2):
                        act.wait_ge(read_d, p.read[j + m][1] + i * p.dd)
                        nc.scalar.activation(hid[s][0][:, m, 0:T], tmp[3 + m][:, 0:T], ACT.Copy).then_inc(hid_hi, 1)

                p = ph["ff_first", l]
                split(p.b + 1, p)
                hidden(p, 0, 0)
                split(p.b + 2, p)
                hidden_hi(p, 2, 0)
                p = ph["ff", l]
                with act.Fori(0, p.turns) as i:
                    for s in range(2):
                        j = 12 * s
                        split(p.b + 3 * s + 1, p, i)
                        hidden(p, j, 0, i)
                        split(p.b + 3 * s + 2, p, i)
                        hidden_hi(p, j + 2, 1 - s, i)
                        split(p.b + 3 * s + 3, p, i)
                p = ph["ff_last", l]
                if l + 1 < DEPTH:
                    split(p.b + 1, p)
                squares(("post_ffn", l), ys, lambda k: act.wait_ge(read_d, p.rd + k + 1))
            p = ph["out"]
            for t in range(SEQ // P):
                copy_out(p, t, rows[:, t, :], D_MODEL)

        @block.vector
        def _(dve):
            def split(b, p, i=0):
                dve.wait_ge(whi_ready, b + 1 + i * p.blocks)
                nc.vector.tensor_tensor(w_lo[:, b % 2, :], stage[:, b % 2, :], w_hi[:, b % 2, :].bitcast(f32),
                                        ALU.subtract).then_inc(wlo_ready, 1)

            def swap(b, p, keys, i=0):
                dve.wait_ge(wlo_ready, b + 1 + i * p.blocks)
                if not keys:
                    nc.vector.tensor_copy(rope_places(w_lo[:, b % 2, :])[1],
                                          rope_places(w_lo[:, b % 2, :].bitcast(f32))[0])
                for half in range(2):
                    src, _ = swap_places(w_lo[:, b % 2, :].bitcast(f32), keys, half)
                    _, dst = swap_places(w_lo[:, b % 2, :], keys, half)
                    last = nc.vector.tensor_copy(dst, src)
                last.then_inc(swap_lo, 1)

            def minus_hi(dst, full, hi):
                return nc.vector.tensor_tensor(dst, full, hi.bitcast(f32), ALU.subtract)

            def stats(key):
                n, p = plan.norms[key], ph[key]
                T = n["T"]
                for k in range(1, n["nk"]):
                    dve.wait_ge(sq_done, n["sq"] + k + 1)
                    if k > 1:
                        dve.wait_ge(sq_added, n["adds"] + k - 1)
                    nc.vector.tensor_tensor(tmp[2][:, 0:T], tmp[0][:, 0:T] if k == 1 else tmp[2][:, 0:T],
                                            tmp[k % 2][:, 0:T], ALU.add).then_inc(sq_added, 1)
                dve.wait_ge(mm_done, p.g + 1)
                nc.vector.tensor_scalar(msq[:, 0:T // P], unit(p.g)[:, 0:T // P],
                                        1.0 / {"q": Q_LORA, "kv": KV_LORA}.get(key[0], D_MODEL), EPS,
                                        ALU.mult, ALU.add).then_inc(read_d, 1)
                dve.wait_ge(rstd_done, n["n"] + 1)
                for t in range(T // P):
                    last = nc.vector.tensor_scalar(tmp[3][:, t * P:(t + 1) * P], ident[:], rstd[:, t:t + 1], None,
                                                   ALU.mult)
                last.then_inc(diag_done, 1)
                dve.wait_ge(mm_done, p.g + 2)

            def scaled(key, src, k, slot=0):
                n = plan.norms[key]
                nc.vector.tensor_tensor(tmp[slot + k % 2][:, 0:n["T"]], src[:, k, 0:n["T"]],
                                        unit(ph[key].g + 1)[:, 0:n["T"]], ALU.mult).then_inc(n_scaled, 1)

            def norm(key, src, lo, hi):
                n = plan.norms[key]
                stats(key)
                scaled(key, src, 0)
                for k in range(n["nk"]):
                    if k + 1 < n["nk"]:
                        scaled(key, src, k + 1)
                    dve.wait_ge(n_hi, n["full"] + k + 1)
                    dve.wait_ge(n_full, n["full"] + k + 1)
                    minus_hi(lo[:, k, 0:n["T"]], tmp[3 + k % 2][:, 0:n["T"]], hi[:, k, 0:n["T"]]
                             ).then_inc(n_lo if k + 1 < n["nk"] else read_d, 1)

            def residual(key):
                n = plan.norms[key]
                stats(key)
                scaled(key, ys, 0, 3)
                for k in range(n["nk"]):
                    if k + 1 < n["nk"]:
                        if k:
                            dve.wait_ge(x_upd, n["upd"] + k)
                        scaled(key, ys, k + 1, 3)
                    dve.wait_ge(n_scaled, n["sq"] + k + 1)
                    for v, (a, b) in enumerate(segs(n["T"])):
                        last = nc.vector.scalar_tensor_tensor(xs[:, k, a:b], tmp[3 + k % 2][:, a:b], scale_of(key, k, v),
                                                              xs[:, k, a:b], ALU.mult, ALU.add)
                    last.then_inc(x_upd if k + 1 < n["nk"] else read_d, 1)

            def ada_columns(l, p, b, j, m0, i):
                for s in range(2):
                    split(b + s + 1, p, i)
                for s in range(2):
                    dve.wait_ge(mm_done, p.g + j + s + 1 + i * p.groups)
                    u = unit(p.g + j + s)[:, 0:4].rearrange("p (m v) -> p m v", v=2)
                    for v in range(2):
                        last = nc.vector.tensor_tensor(mods[:, ds(m0 + 2 * s, 2), v], u[:, :, v],
                                                       vecs[:, l, ds(m0 + 2 * s, 2)], ALU.add)
                    last.then_inc(read_d, 1)

            def gains(l, which):
                for n in which:
                    name, m, plus = (("g_pre_mix", 0, 1.0), ("g_post_mix", 2 * DT, 0.0), ("g_pre_ffn", 3 * DT, 1.0),
                                     ("g_post_ffn", 5 * DT, 0.0))[n]
                    g = vecs[:, l, vec[name][0]:vec[name][1]]
                    for v in range(2):
                        last = nc.vector.scalar_tensor_tensor(gain[:, n, :, v], mods[:, m:m + DT, v], plus, g,
                                                              ALU.add, ALU.mult)
                last.then_inc(mods_step, 1)

            def rotate(count, cos_j, p, T, i=0):
                u, w = unit(p.g + cos_j), unit(p.g + cos_j + 1)
                dve.wait_ge(mm_done, p.g + cos_j + 1 + i * p.groups)
                last = nc.vector.tensor_tensor(tmp[3][:, 0:SEQ], u[:, 0:SEQ], rope_t[:, 0, :], ALU.mult)
                if T > SEQ:
                    last = nc.vector.tensor_copy(tmp[2][:, SEQ:TOK], u[:, SEQ:TOK])
                last.then_inc(read_d, 1)
                dve.wait_ge(mm_done, p.g + cos_j + 2 + i * p.groups)
                nc.vector.tensor_tensor(tmp[4][:, 0:SEQ], w[:, 0:SEQ], rope_t[:, 1, :], ALU.mult).then_inc(read_d, 1)
                dve.wait_ge(read_d, p.read[cos_j + 1][1] + i * p.dd)
                nc.vector.tensor_tensor(tmp[2][:, 0:SEQ], tmp[3][:, 0:SEQ], tmp[4][:, 0:SEQ], ALU.add
                                        ).then_inc(rope_sum, 1)

            for l in range(DEPTH):
                dve.wait_ge(mm_done, l + 1)
                nc.vector.tensor_copy(vecs[:, l, :], unit(l)[:, 0:n_vec]).then_inc(read_d, 1)
            split(0, ph["ada", 0])
            dve.wait_ge(c_ready, 3)
            for v in range(2):
                cols = cst[:, 0:DT * 4].rearrange("p (k f) -> p k f", f=4)
                last = minus_hi(cols[:, :, 2 * v + 1], csil[:, v * DT:(v + 1) * DT], cols[:, :, 2 * v])
            last.then_inc(c_ready, 1)
            dve.wait_ge(ident_in, 16)
            dve.wait_ge(consts_in, 48)
            for l in range(DEPTH):
                T = tokens(l)
                p = ph["ada", l]
                with dve.Fori(0, p.turns) as i:
                    ada_columns(l, p, p.b, 2, 4 * i, i)
                dve.wait_ge(read_d, p.rd + p.turns * p.dd)
                gains(l, (0,))
                dve.wait_ge(mods_step, 2 * l + 1)
                norm(("pre_mix", l), xs, h[1], h[0])
                p = ph["u", l]
                split(p.b + 1, p)
                split(p.b + 2, p)
                p = ph["qkv", l]
                split(p.b + 1, p)
                split(p.b + 2, p)
                swap(p.b + 2, p, True)
                split(p.b + 3, p)
                rotate(0, 3, p, TOK)
                dve.wait_ge(rope_hi, 1 + l * (PAIRS + 1))
                minus_hi(kr[1][:, 0, :], tmp[2][:, :], kr[0][:, 0, :]).then_inc(rope_lo, 1)
                for half in range(2):
                    p = ph["g%d" % half, l]
                    if half == 1:
                        for g in range(NG):
                            dve.wait_ge(pd_hi, NG * l + g + 1)
                            for v, (a, b) in enumerate(segs(T)):
                                off = U_C - SEQ if v else U_X
                                last = minus_hi(pd[1][:, g, a:b], u_pad[:, g, a + off:b + off], pd[0][:, g, a:b])
                            last.then_inc(pd_lo, 1)
                        norm(("q", l), raw[:, 0:2, :], ql[1], ql[0])
                        norm(("kv", l), raw[:, 2:3, :], kvl[1], kvl[0])
                    with dve.Fori(0, p.turns) as i:
                        for s in range(2):
                            split(p.b + s + 1, p, i)
                p = ph["w_pool", l]
                split(p.b + 1, p)
                a = vec["pool_scale"][0]
                for g in range(NG):
                    dve.wait_ge(wp_hi, NG * l + g + 1)
                    nc.vector.scalar_tensor_tensor(pd[1][:, g, 0:T], unit(p.g + g)[:, 0:T],
                                                   vecs[:, l, a + g:a + g + 1], pd[0][:, g, 0:T].bitcast(f32),
                                                   ALU.mult, ALU.subtract).then_inc(read_d, 1)
                p = ph["w_o_pool", l]
                for s in range(2):
                    split(p.b + s + 1, p)
                    for m in range(4):
                        j = 4 * s + m
                        dve.wait_ge(mm_done, p.g + j + 1)
                        nc.vector.tensor_tensor(ys[:, j, 0:T], unit(p.g + j)[:, 0:T], ys[:, j, 0:T], ALU.mult
                                                ).then_inc(read_d, 1)
                p = ph["pairs", l]
                order = attention_order(l)
                with dve.Fori(0, p.turns) as i:
                    def lo_of(j, n, dst, src, hi):
                        dve.wait_ge(proj_hi, after(N_PROJ, l, i, n))
                        minus_hi(dst, src, hi).then_inc(read_d, 1)
                    swap(p.b, p, False, i)
                    split(p.b + 1, p, i)
                    for hd in range(2):
                        lo_of(hd, hd + 1, qn[1][:, hd, 0:T], unit(p.g + hd)[:, 0:T], qn[0][:, hd, 0:T])
                    rotate(0, 2, p, T, i)
                    dve.wait_ge(rope_hi, 2 + l * (PAIRS + 1) + i)
                    minus_hi(qr[1][:, 0, 0:T], tmp[2][:, 0:T], qr[0][:, 0, 0:T]).then_inc(rope_lo, 1)
                    for hd in range(2):
                        lo_of(4 + hd, 3 + hd, kn[1][:, hd, :], unit(p.g + 4 + hd)[:, 0:TOK], kn[0][:, hd, :])
                    for j, (a, b) in enumerate(V_TILES[l]):
                        lo_of(6 + j, 5 + j, vv[1][:, a:b, :], as_values(unit(p.g + 6 + j), b - a), vv[0][:, a:b, :])
                    j0 = 6 + len(V_TILES[l])
                    ada_columns(l, p, p.b + 1, j0 + 2, 16 + 8 * i, i)
                    j0 += 4

                    def probabilities(t):
                        where = [n for n, o in enumerate(order) if o == ("S", t)][0]
                        dve.wait_ge(read_a, p.read[j0 + where][1] + i * p.da)
                        places = score_places(l, t, unit(0))
                        w = len(places)
                        nc.vector.reciprocal(st[:, t % 2, 6:6 + w], st[:, t % 2, 4:4 + w]).then_inc(p_norm, 1)
                        dve.wait_ge(p_norm, after(N_STAT, l, i, 2 * t + 1))
                        for v, (_, e) in enumerate(places):
                            last = nc.vector.tensor_scalar(e, e, st[:, t % 2, 6 + v:7 + v], None, ALU.mult)
                        last.then_inc(p_norm, 1)

                    n_pv = 0
                    for n, (kind, t) in enumerate(order):
                        u = unit(p.g + j0 + n)
                        if kind == "S":
                            dve.wait_ge(mm_done, p.g + j0 + n + 1 + i * p.groups)
                            places = score_places(l, t, u)
                            w = len(places)
                            src = u if w == 1 else u.rearrange("p (v k) -> p v k", v=2)
                            nc.vector.reduce_max(st[:, t % 2, 0:w], src[:, 0:TOK] if w == 1 else src[:, :, 0:CTX], AX.X
                                                 ).then_inc(smax, 1)
                            dve.wait_ge(smax, after(N_STAT, l, i, 2 * t + 1))
                            nc.vector.tensor_scalar(st[:, t % 2, 2:2 + w], st[:, t % 2, 0:w], -SCALE, None, ALU.mult
                                                    ).then_inc(smax, 1)
                            if t >= 1:
                                probabilities(t - 1)
                        elif kind == "T":
                            if t == N_TILES[l] - 2:
                                probabilities(t + 1)
                            dve.wait_ge(pt_hi, after(N_TILES, l, i, t + 1))
                            src, dst = turned_places(l, t, u)
                            minus_hi(dst[1], src, dst[0]).then_inc(read_d, 1)
                        else:
                            hd, a, _ = pv_place(l, t)
                            dve.wait_ge(o_hi, after(N_PV, l, i, t + 1))
                            minus_hi(oo[1][:, hd, a:a + 256], u[:, 0:256], oo[0][:, hd, a:a + 256]).then_inc(read_d, 1)
                    j0 += len(order)
                    ada_columns(l, p, p.b + 3, j0 + 2, 20 + 8 * i, i)
                    split(p.b + 6, p, i)
                    j0 += 4
                    for m in range(DT):
                        dve.wait_ge(mm_done, p.g + j0 + m + 1 + i * p.groups)
                        nc.vector.tensor_tensor(tmp[m % 2][:, 0:T], unit(p.g + j0 + m)[:, 0:T], xs[:, m, 0:T], ALU.mult
                                                ).then_inc(read_d, 1)
                        dve.wait_ge(read_d, p.read[j0 + m][1] + i * p.dd)
                        nc.vector.tensor_tensor(ys[:, m, 0:T], ys[:, m, 0:T], tmp[m % 2][:, 0:T], ALU.add
                                                ).then_inc(merged_add, 1)
                gains(l, (1, 2, 3))
                for k in range(DT):
                    dve.wait_ge(mg_hi, DT * l + k + 1)
                    minus_hi(mg[1][:, k, 0:T], ys[:, k, 0:T], mg[0][:, k, 0:T]).then_inc(mg_lo, 1)
                p = ph["w_out", l]
                with dve.Fori(0, p.turns) as i:
                    for s in range(2):
                        split(p.b + s + 1, p, i)
                dve.wait_ge(mods_step, 2 * l + 2)
                dve.wait_ge(x_back, 16 * (l + 1))
                residual(("post_mix", l))
                norm(("pre_ffn", l), xs, h[1], h[0])

                def times_up(p, j, n, i=0):
                    for m in range(2):
                        dve.wait_ge(silu_done, n + m + 1 + 4 * i)
                        dve.wait_ge(mm_done, p.g + j + m + 1 + i * p.groups)
                        nc.vector.tensor_tensor(tmp[3 + m][:, 0:T], unit(p.g + j + m)[:, 0:T], tmp[m][:, 0:T],
                                                ALU.mult).then_inc(read_d, 1)

                def hidden_lo(s, n, i=0):
                    for m in range(2):
                        dve.wait_ge(hid_hi, n + m + 1 + 4 * i)
                        minus_hi(hid[s][1][:, m, 0:T], tmp[3 + m][:, 0:T], hid[s][0][:, m, 0:T]).then_inc(hid_lo, 1)

                def add_y(p, j, i=0):
                    for m in range(DT):
                        dve.wait_ge(mm_done, p.g + j + m + 1 + i * p.groups)
                        nc.vector.tensor_tensor(ys[:, m, 0:T], unit(p.g + j + m)[:, 0:T], ys[:, m, 0:T], ALU.add
                                                ).then_inc(read_d, 1)

                n0 = 2 * FF_GROUPS * l
                p = ph["ff_first", l]
                split(p.b + 1, p)
                split(p.b + 2, p)
                times_up(p, 2, n0)
                hidden_lo(0, n0)
                dve.wait_ge(y_clear, l + 1)
                p = ph["ff", l]
                with dve.Fori(0, p.turns) as i:
                    for s in range(2):
                        j = 12 * s
                        split(p.b + 3 * s + 1, p, i)
                        split(p.b + 3 * s + 2, p, i)
                        times_up(p, j + 2, n0 + 2 + 2 * s, i)
                        hidden_lo(1 - s, n0 + 2 + 2 * s, i)
                        split(p.b + 3 * s + 3, p, i)
                        add_y(p, j + 4, i)
                p = ph["ff_last", l]
                if l + 1 < DEPTH:
                    split(p.b + 1, p)
                add_y(p, 0)
                residual(("post_ffn", l))

        @block.tensor
        def _(pe):
            def product(g, weights, moving, n_k, n_tok, ready=None):
                for a, b in segs(n_tok):
                    for k in range(n_k):
                        if ready and a == 0:
                            ready(k)
                        (wh, wl), (mh, ml) = weights(k), moving(k, a, b)
                        out_u = unit(g)[:, a:b]
                        nc.tensor.matmul(out_u, wh, mh, start=k == 0, stop=False)
                        nc.tensor.matmul(out_u, wh, ml, start=False, stop=False)
                        last = nc.tensor.matmul(out_u, wl, mh, start=False, stop=k == n_k - 1)
                return last

            def take(p, j, i=0):
                e, n = freed(p, j, i) if (p.turns > 1 or j >= 4) else (None, None)
                if e is not None:
                    pe.wait_ge(e, n)

            def drained(p):
                if p.ra:
                    pe.wait_ge(read_a, p.ra)
                if p.rd:
                    pe.wait_ge(read_d, p.rd)

            def have(b, p, i=0):
                pe.wait_ge(wlo_ready, b + 1 + i * p.blocks)

            def cols(b, k, width, m, n=P):
                a = k * width + m
                return w_hi[:, b % 2, a:a + n], w_lo[:, b % 2, a:a + n]

            def both(x2, k, a, b):
                return x2[0][:, k, a:b], x2[1][:, k, a:b]

            def stats(key):
                n, p = plan.norms[key], ph[key]
                T = n["T"]
                drained(p)
                if n["nk"] > 1:
                    pe.wait_ge(sq_added, n["adds"] + n["nk"] - 1)
                else:
                    pe.wait_ge(sq_done, n["sq"] + 1)
                total = tmp[2] if n["nk"] > 1 else tmp[0]
                for t in range(T // P):
                    last = nc.tensor.matmul(unit(p.g)[:, t:t + 1], total[:, t * P:(t + 1) * P], ones[:, 0:1],
                                            start=True, stop=True)
                last.then_inc(mm_done, 1)
                pe.wait_ge(diag_done, n["n"] + 1)
                for a, b in segs(T):
                    last = nc.tensor.matmul(unit(p.g + 1)[:, a:b], ones[:], tmp[3][:, a:b], start=True, stop=True)
                last.then_inc(mm_done, 1)

            def normed(key):
                n = plan.norms[key]

                def ready(k):
                    if k < n["nk"] - 1:
                        pe.wait_ge(n_lo, n["rest"] + k + 1)
                    else:
                        pe.wait_ge(read_d, ph[key].read[1][1])
                return ready

            def ada_rows(p, b, j, i):
                for s in range(2):
                    have(b + s, p, i)
                    take(p, j + s, i)
                    for k in range(DT):
                        c4 = cst[:, 4 * k:4 * k + P]
                        wh, wl = cols(b + s, k, 256, 0, 256)
                        nc.tensor.matmul(unit(p.g + j + s)[:, 0:256], c4, wh, start=k == 0, stop=False)
                        last = nc.tensor.matmul(unit(p.g + j + s)[:, 0:256], c4, wl, start=False, stop=k == DT - 1)
                    last.then_inc(mm_done, 1)
                for s in range(2):
                    pe.wait_ge(read_a, p.read[j + s][1] + i * p.da)
                    take(p, j + 2 + s, i)
                    for m in range(2):
                        last = nc.tensor.matmul(unit(p.g + j + 2 + s)[:, 2 * m:2 * m + 2],
                                                mrow[:, s, m * P:(m + 1) * P], pair_sum[:], start=True, stop=True)
                    last.then_inc(mm_done, 1)

            def full_block(b, p, j, moving, n_tok, i=0, ready=None, width=256, tiles=2, n_k=DT):
                have(b, p, i)
                for m in range(tiles):
                    take(p, j + m, i)
                    product(p.g + j + m, lambda k: cols(b, k, width, m * P), moving, n_k, n_tok,
                            ready if m == 0 else None).then_inc(mm_done, 1)

            pe.wait_ge(ident_in, 16)
            pe.wait_ge(rows_in, 16 * len(VEC_ROWS) * DEPTH)
            for l in range(DEPTH):
                nc.tensor.transpose(unit(l)[:, 0:n_vec], vrow[l][0:n_vec, :], ident[0:n_vec, 0:n_vec]
                                    ).then_inc(mm_done, 1)
            p = ph["x_in"]
            pe.wait_ge(x_in, 16 * (TOK // P))
            drained(p)
            for k in range(DT):
                take(p, k)
                for t in range(TOK // P):
                    last = nc.tensor.transpose(unit(p.g + k)[:, t * P:(t + 1) * P], rows[:, t, k * P:(k + 1) * P],
                                               ident[:])
                last.then_inc(mm_done, 1)
            pe.wait_ge(c_ready, 4)
            pe.wait_ge(cleared, 4)
            pe.wait_ge(consts_in, 48)
            for l in range(DEPTH):
                T = tokens(l)
                p = ph["ada", l]
                drained(p)
                with pe.Fori(0, p.turns) as i:
                    ada_rows(p, p.b, 0, i)
                stats(("pre_mix", l))

                def hs(k, a, b):
                    return both(h, k, a, b)
                p = ph["u", l]
                drained_rows = normed(("pre_mix", l))
                full_block(p.b, p, 0, hs, T, ready=drained_rows)
                full_block(p.b + 1, p, 2, hs, T)
                p = ph["qkv", l]
                drained(p)
                full_block(p.b, p, 0, hs, T)
                full_block(p.b + 1, p, 2, hs, TOK, width=128, tiles=1)
                have(p.b + 2, p)
                for m in range(2):
                    take(p, 3 + m)
                    if m == 1:
                        pe.wait_ge(swap_hi, 1 + l * (PAIRS + 1))
                        pe.wait_ge(swap_lo, 1 + l * (PAIRS + 1))
                    product(p.g + 3 + m, lambda k: cols(p.b + 2, k, 256, m * P), hs, DT, TOK).then_inc(mm_done, 1)
                for half in range(2):
                    if half == 1:
                        stats(("q", l))
                        stats(("kv", l))
                    p = ph["g%d" % half, l]
                    drained(p)
                    with pe.Fori(0, p.turns) as i:
                        for s in range(2):
                            full_block(p.b + s, p, 2 * s, hs, T, i)
                p = ph["w_pool", l]
                drained(p)
                have(p.b, p)
                pe.wait_ge(pd_lo, NG * (l + 1))
                for g in range(NG):
                    product(p.g + g, lambda k: cols(p.b, g, P, 0), lambda k, a, b: both(pd, g, a, b), 1, T
                            ).then_inc(mm_done, 1)
                p = ph["w_o_pool", l]
                drained(p)
                for s in range(2):
                    full_block(p.b + s, p, 4 * s, lambda k, a, b: both(pd, k, a, b), T, width=512, tiles=4, n_k=4)
                p = ph["pairs", l]
                drained(p)
                with pe.Fori(0, p.turns) as i:
                    b0 = p.b % 2
                    have(p.b, p, i)
                    for hd in range(2):
                        take(p, hd, i)
                        product(p.g + hd, lambda k: cols(b0, k, 384, hd * (NOPE + ROPE)),
                                lambda k, a, b: both(ql, k, a, b), 2, T).then_inc(mm_done, 1)

                    take(p, 2, i)
                    pe.wait_ge(swap_hi, 2 + l * (PAIRS + 1) + i)
                    pe.wait_ge(swap_lo, 2 + l * (PAIRS + 1) + i)
                    product(p.g + 2, lambda k: cols(b0, k, P, 1280), lambda k, a, b: both(ql, k, a, b), 2, T).then_inc(mm_done, 1)
                    take(p, 3, i)
                    product(p.g + 3, lambda k: cols(b0, k, P, 1536), lambda k, a, b: both(ql, k, a, b), 2, T
                            ).then_inc(mm_done, 1)
                    for hd in range(2):
                        take(p, 4 + hd, i)
                        product(p.g + 4 + hd, lambda k: cols(b0, 0, 0, 768 + hd * 256),
                                lambda k, a, b: both(kvl, 0, a, b), 1, TOK).then_inc(mm_done, 1)
                    wv = [w[:, b0, 768:1280].rearrange("p (h n) -> p h n", h=2)[:, :, NOPE:] for w in (w_hi, w_lo)]
                    for j, (t0, t1) in enumerate(V_TILES[l]):
                        take(p, 6 + j, i)
                        for t in range(t0, t1):
                            o_v = unit(p.g + 6 + j)[:, (t - t0) * 256:(t - t0 + 1) * 256]
                            kh, kl = (kvl[n][:, 0, t * P:(t + 1) * P] for n in range(2))
                            nc.tensor.matmul(o_v, kh, wv[0], start=True, stop=False)
                            nc.tensor.matmul(o_v, kh, wv[1], start=False, stop=False)
                            last = nc.tensor.matmul(o_v, kl, wv[0], start=False, stop=True)
                        last.then_inc(mm_done, 1)
                    j0 = 6 + len(V_TILES[l])
                    ada_rows(p, p.b + 1, j0, i)
                    j0 += 4
                    pe.wait_ge(rope_lo, 2 + l * (PAIRS + 1) + i)
                    pe.wait_ge(read_d, p.read[j0 - 5][1] + i * p.dd)
                    tiles, sets = attention_tiles(l), pv_sets(l)
                    for n, (kind, t) in enumerate(attention_order(l)):
                        u = unit(p.g + j0 + n)
                        take(p, j0 + n, i)
                        if kind == "S":
                            hd, m, of_ctx = tiles[t]
                            todo = ([(SEQ + v * P, v * SEQ, SEQ, TOK) for v in range(2)] if of_ctx else
                                    [(m * P, a, a, b) for a, b in segs(TOK)])
                            r = slice(hd * ROPE, (hd + 1) * ROPE)
                            for q0, o0, k0, k1 in todo:
                                o_s = u[:, o0:o0 + k1 - k0]
                                qh, qlo = (qn[n2][:, hd, q0:q0 + P] for n2 in range(2))
                                kh, klo = (kn[n2][:, hd, k0:k1] for n2 in range(2))
                                nc.tensor.matmul(o_s, qh, kh, start=True, stop=False)
                                nc.tensor.matmul(o_s, qh, klo, start=False, stop=False)
                                nc.tensor.matmul(o_s, qlo, kh, start=False, stop=False)
                                qh, qlo = (qr[n2][r, 0, q0:q0 + P] for n2 in range(2))
                                kh, klo = (kr[n2][r, 0, k0:k1] for n2 in range(2))
                                nc.tensor.matmul(o_s, qh, kh, start=False, stop=False)
                                nc.tensor.matmul(o_s, qh, klo, start=False, stop=False)
                                last = nc.tensor.matmul(o_s, qlo, kh, start=False, stop=True)
                        elif kind == "T":
                            pe.wait_ge(p_norm, after(N_STAT, l, i, 2 * t + 2))
                            e = tmp[3 + t % 2]
                            if tiles[t][2]:
                                todo = [(k * CTX + v * P, v * CTX + k * P) for v in range(2) for k in range(2)]
                            else:
                                todo = [(k * P, k * P) for k in range(KT_ALL)]
                            for o0, e0 in todo:
                                last = nc.tensor.transpose(u[:, o0:o0 + P], e[:, e0:e0 + P], ident[:])
                        else:
                            own = next(o for k, o in sets.values() if k == t)
                            where = [n3 for n3, o in enumerate(attention_order(l)) if o == ("T", own[-1])][0]
                            pe.wait_ge(read_d, p.read[j0 + where][1] + i * p.dd)
                            hd, _, k0 = pv_place(l, t)
                            n_k = KT_ALL - k0
                            for k in range(n_k):
                                vh, vl = (vv[n2][:, k0 + k, hd * V_DIM:(hd + 1) * V_DIM] for n2 in range(2))
                                ph_, pl = (pt[t % 2][n2][:, k, :] for n2 in range(2))
                                nc.tensor.matmul(u[:, 0:256], vh, ph_, start=k == 0, stop=False)
                                nc.tensor.matmul(u[:, 0:256], vh, pl, start=False, stop=False)
                                last = nc.tensor.matmul(u[:, 0:256], vl, ph_, start=False, stop=k == n_k - 1)
                        last.then_inc(mm_done, 1)
                    j0 += len(attention_order(l))
                    ada_rows(p, p.b + 3, j0, i)
                    pe.wait_ge(read_d, p.read[j0 - 1][1] + i * p.dd)
                    full_block(p.b + 5, p, j0 + 4, lambda k, a, b: both(oo, k, a, b), T, i, width=D_MODEL,
                               tiles=DT, n_k=2)
                p = ph["w_out", l]
                drained(p)
                pe.wait_ge(mg_lo, DT * (l + 1))
                with pe.Fori(0, p.turns) as i:
                    for s in range(2):
                        full_block(p.b + s, p, 2 * s, lambda k, a, b: both(mg, k, a, b), T, i)
                stats(("post_mix", l))
                stats(("pre_ffn", l))
                p = ph["ff_first", l]
                rows_ready = normed(("pre_ffn", l))
                full_block(p.b, p, 0, hs, T, ready=rows_ready)
                full_block(p.b + 1, p, 2, hs, T)
                n0 = 2 * FF_GROUPS * l

                def down(b, p, j, s, i=0):
                    full_block(b, p, j, lambda k, a, b: both(hid[s], k, a, b), T, i, width=D_MODEL, tiles=DT, n_k=2)
                p = ph["ff", l]
                drained(p)
                with pe.Fori(0, p.turns) as i:
                    for s in range(2):
                        j = 12 * s
                        full_block(p.b + 3 * s, p, j, hs, T, i)
                        full_block(p.b + 3 * s + 1, p, j + 2, hs, T, i)
                        pe.wait_ge(hid_lo, n0 + 2 + 2 * s + 4 * i)
                        down(p.b + 3 * s + 2, p, j + 4, s, i)
                p = ph["ff_last", l]
                drained(p)
                pe.wait_ge(hid_lo, n0 + 2 * FF_GROUPS)
                down(p.b, p, 0, 0)
                stats(("post_ffn", l))
            p = ph["out"]
            drained(p)
            for t in range(SEQ // P):
                for k in range(DT):
                    last = nc.tensor.transpose(unit(p.g + t)[:, k * P:(k + 1) * P], xs[:, k, t * P:(t + 1) * P],
                                               ident[:])
                last.then_inc(mm_done, 1)


_INS = ['x', 'c', 'ctx', 'c_ctx', 'w_ada', 'b_ada', 'g_pre_mix', 'w_in', 'q_norm', 'w_uq', 'kv_norm', 'w_ukv',
        'w_o_mla', 'w_pool', 'pool_scale', 'w_o_pool', 'w_out', 'g_post_mix', 'g_pre_ffn', 'w_ffn_gate',
        'w_ffn_up', 'w_ffn_down', 'g_post_ffn']
_OUTS = [((1, 512, 1024), 'float32')]


def shape_constants():
    import numpy as np
    ident = np.eye(P, dtype=np.float32)
    pos = np.stack([np.arange(SEQ) // GRID_W, np.arange(SEQ) % GRID_W]).astype(np.float32)
    axis = ROPE // 2
    freq = np.float32(THETA) ** (-np.arange(0, axis, 2, dtype=np.float32) / np.float32(axis))
    ang = (pos[:, None, :] * freq[None, :, None]).astype(np.float32)
    cos, sin = np.cos(ang), np.sin(ang)
    cos = np.stack([cos, cos], 1).reshape(ROPE, SEQ)
    sin = np.stack([-sin, sin], 1).reshape(ROPE, SEQ)
    rope = np.stack([np.tile(cos, (2, 1)), np.tile(sin, (2, 1))], 1).astype(np.float32)
    edge = np.ones((NG, 2, 2, PAD), np.float32)
    for g, w in enumerate(WINDOWS):
        for t, n in enumerate((SEQ, CTX)):
            q = np.arange(n)
            count = np.clip(q + w - w // 2, 0, n) - np.clip(q - w // 2, 0, n)
            edge[g, 0, t], edge[g, 1, t] = w / count[:PAD], w / count[-PAD:]
    edge = np.ascontiguousarray(np.broadcast_to(edge, (P,) + edge.shape))
    pair = np.array([[1, 0], [1, 0], [0, 1], [0, 1]], np.float32)
    return {"k_ident": ident, "k_rope": rope, "k_edge": edge, "k_pair": pair}


def kernel(**inputs):
    import numpy as _np
    import concourse.bacc as _bacc
    from concourse import mybir as _mybir
    from concourse.bass_utils import run_bass_kernel_spmd as _run

    nc = _bacc.Bacc("TRN2", target_bir_lowering=False, num_devices=1, dynamic_dma_scratch_size=256)
    arrays, args = {}, []
    consts = shape_constants()
    for name in _INS + list(consts):
        a = _np.ascontiguousarray(inputs[name] if name in inputs else consts[name])
        arrays[f"in_{name}_dram"] = a
        args.append(nc.dram_tensor(f"in_{name}_dram", a.shape, _mybir.dt.from_np(a.dtype), kind="ExternalInput").ap())
    for i, (shape, dtype) in enumerate(_OUTS):
        dt = _mybir.dt.from_np(_np.dtype(dtype))
        args.append(nc.dram_tensor(f"out_{i}_dram", shape, dt, kind="ExternalOutput").ap())
    args.append(nc.dram_tensor("x_keep", (P, DT, TOK), _mybir.dt.float32, kind="Internal").ap())
    backbone_kernel(nc, *args)
    r = _run(nc, [arrays], core_ids=[0])
    got = tuple(r.results[0][f"out_{i}_dram"] for i in range(len(_OUTS)))
    return got[0]
```

```python
from contextlib import ExitStack

import concourse.bass as bass
from concourse import mybir

P = 128
D_MODEL, SEQ, CTX, DEPTH = 1024, 512, 256, 2
HEADS, NOPE, ROPE, V_DIM = 8, 128, 64, 128
Q_LORA, KV_LORA, POOL_W, D_FF = 256, 128, 512, 2816
OFF_KV = Q_LORA
OFF_KR = OFF_KV + KV_LORA
OFF_POOL = OFF_KR + ROPE
OFF_GATE = OFF_POOL + POOL_W
GRID_W, THETA, EPS = 64, 10000.0, 1e-6
SCALE = float(NOPE + ROPE) ** -0.5

TOK = SEQ + CTX
DT = D_MODEL // P
KT_ALL = TOK // P
BLK = 2048
UNIT = 1024
WINDOWS = (2, 4, 8, 16)
NG = len(WINDOWS)
PAD = 8
U_LEN = PAD + SEQ + PAD + CTX + PAD
U_X, U_C = PAD, PAD + SEQ + PAD
FF_GROUPS = D_FF // 256
FF_TURNS = (FF_GROUPS - 1) // 2
ADA_TURNS = 2 * DT * P // 512
PAIRS = HEADS // 2

VEC_ROWS = (("b_ada", 48), ("g_pre_mix", 8), ("g_post_mix", 8), ("g_pre_ffn", 8), ("g_post_ffn", 8),
            ("q_norm", 2), ("kv_norm", 1), ("pool_scale", 4), ("c", 8), ("c_ctx", 8))


def vec_columns():
    at, out = 0, {}
    for name, n in VEC_ROWS:
        out[name] = (at, at + n)
        at += n
    return out, at


class Phase:

    def __init__(self, plan, blocks, units, turns):
        self.b, self.g, self.ra, self.rd = plan.b, plan.g, plan.ra, plan.rd
        self.blocks, self.groups, self.turns = blocks, len(units), turns
        self.free_at = []
        a = d = 0
        for r in units:
            if r == "A":
                a += 1
            if r == "D":
                d += 1
            self.free_at.append(("A", plan.ra + a + (r == "a")) if r in "Aa" else ("D", plan.rd + d + (r == "d")))
        self.da, self.dd = a, d
        plan.b += blocks * turns
        plan.g += len(units) * turns
        plan.ra += a * turns
        plan.rd += d * turns


class Plan:

    def __init__(self):
        self.b = self.g = self.ra = self.rd = 0
        self.ph = {}
        self.free_counts = []
        self.end = {}
        self.norms = {}
        self.adds = self.nk_all = self.upd = self.lo_all = self.full = self.n_norm = 0

        def add(key, blocks, units, turns=1, ends=()):
            p = self.ph[key] = Phase(self, blocks, units, turns)
            for t in range(turns):
                self.free_counts += [(e, n + t * (p.da if e == "A" else p.dd)) for e, n in p.free_at]
                for j, e in enumerate(ends):
                    self.end[p.b + t * blocks + j] = p.g + t * len(units) + e

        def norm(key, nk, tokens, post=False, apart=False):
            self.norms[key] = dict(nk=nk, T=tokens, adds=self.adds, sq=self.nk_all, rest=self.lo_all, full=self.full,
                                   upd=self.upd, n=self.n_norm)
            self.adds += nk if post or key == ("pre_mix", 0) else nk - 1
            self.nk_all += nk
            self.n_norm += 1
            if post:
                self.upd += nk - 1
            else:
                self.lo_all += nk - 1
                self.full += nk
            if not apart:
                add(key, 0, "DD")
                places(key, (key, 0), (key, 1))

        def places(key, *at):
            self.norms[key]["at"] = [(self.ph[k].g + j, self.ph[k].free_at[j][1]) for k, j in at]

        add("vectors", 0, "D" * DEPTH)
        add(("ada_first", 0), 2, "AADD", 1, (1, 2))
        add("x_in", 0, "A" * DT)
        for l in range(DEPTH):
            T = TOK if l == 0 else SEQ
            norm(("pre_mix", l), DT, TOK, apart=l == 0)
            if l == 0:
                add(("x_sums", l), 0, "D")
                add(("ada", l), 2, "AADD", ADA_TURNS - 1, (1, 2))
                add(("x_spread", l), 0, "D")
                places(("pre_mix", l), (("x_sums", l), 0), (("x_spread", l), 0))
            add(("u", l), 2, "AAAA", 1, (2, 4))
            add(("qkv", l), 3, "DDDDD", 1, (2, 3, 5))
            add(("g0", l), 2, "AAAA", 2, (2, 4))
            norm(("q", l), 2, T, apart=True)
            norm(("kv", l), 1, TOK, apart=True)
            add(("sums", l), 0, "DD")
            add(("g1", l), 2, "AAAA", 2, (2, 4))
            add(("w_pool", l), 1, "DDDD", 1, (4,))
            add(("w_o_pool", l), 2, "D" * 10, 1, (4, 10))
            places(("q", l), (("sums", l), 0), (("w_o_pool", l), 4))
            places(("kv", l), (("sums", l), 1), (("w_o_pool", l), 5))
            nv = 4 if l == 0 else 2
            seq = attention_groups(l)
            kinds = "".join("A" if k in "SR" else "D" for k, _ in seq)
            n0 = 6 + nv
            row_ends = [n0 + seq.index(("R", s)) + 1 for s in range(4)]
            add(("pairs", l), 6, "D" * n0 + kinds + "D" * 8, PAIRS, [n0] + row_ends + [n0 + len(seq) + 8])
            add(("w_out", l), 2, "AAAA", 2, (2, 4))
            norm(("post_mix", l), DT, T, True)
            norm(("pre_ffn", l), DT, T)
            add(("ff_first", l), 2, "dDdD", 1, (2, 4))
            plain = "dDdD" + "D" * 8
            if l + 1 < DEPTH:
                add(("ff_ada", l), 6, ("dDdD" + "A" + "D" * 8 + "D") * 2, ADA_TURNS, (2, 4, 13, 16, 18, 27))
                add(("ff", l), 6, plain * 2, FF_TURNS - ADA_TURNS, (2, 4, 12, 14, 16, 24))
            else:
                add(("ff", l), 6, plain * 2, FF_TURNS, (2, 4, 12, 14, 16, 24))
            add(("ff_last", l), 1, "D" * 8, 1, (8,))
            norm(("post_ffn", l), DT, T, True)
        add("out", 0, "ADAD")


def attention_tiles(l):
    out = []
    for h in range(2):
        out += [(h, n, False) for n in range(SEQ // P)]
        if l == 0:
            out.append((h, 0, True))
    return out


def pv_sets(l):
    out, now = {}, []
    for t, (h, n, c) in enumerate(attention_tiles(l)):
        now.append(t)
        if c or len(now) == 2:
            out[t] = (len(out), tuple(now))
            now = []
    return out


def attention_order(l):
    n, sets, waiting = len(attention_tiles(l)), pv_sets(l), []
    out = [("R", 0), ("S", 0), ("S", 1), ("S", 2), ("C", 0)]
    behind = {2: ["R1"], 3: ["C1"], n - 3: ["R2"], n - 1: ["L5", "R3"]}
    hi = {0: 2, 1: 3, n - 4: 4, n - 1: 5}
    for t in range(n):
        out.append(("T", t))
        if t in hi:
            out.append(("H", hi[t]))
        if t + 3 < n:
            out.append(("S", t + 3))
        if waiting:
            out.append(("V", waiting.pop()))
        out += [(k[0], int(k[1])) for k in behind.get(t, [])]
        if t in sets:
            waiting.append(sets[t][0])
    return out + [("V", waiting.pop()), ("C", 2), ("C", 3), ("H", 6)]


def attention_groups(l):
    return [o for o in attention_order(l) if o[0] not in "HL"]


def backbone_kernel(nc, x, c, ctx, c_ctx, w_ada, b_ada, g_pre_mix, w_in, q_norm, w_uq, kv_norm, w_ukv, w_o_mla,
                    w_pool, pool_scale, w_o_pool, w_out, g_post_mix, g_pre_ffn, w_ffn_gate, w_ffn_up,
                    w_ffn_down, g_post_ffn, k_ident, k_rope, k_edge, k_pair, out, x_keep):
    f32, f32r = mybir.dt.float32, mybir.dt.float32r
    ACT, ALU, AX = mybir.ActivationFunctionType, mybir.AluOpType, mybir.AxisListType
    ds = bass.ds
    plan = Plan()
    ph = plan.ph
    vec, n_vec = vec_columns()
    es = ExitStack()
    with es:
        def sb(name, shape, dt=f32):
            return es.enter_context(nc.sbuf_tensor(name, shape, dt))

        def sem(name):
            return es.enter_context(nc.semaphore(name))

        stage = sb("stage", [P, 2, BLK])
        w_hi = sb("w_hi", [P, 2, BLK], f32r)
        w_lo = sb("w_lo", [P, 2, BLK], f32r)
        HT, QT = DT * TOK, 6 * TOK
        arena = sb("arena", [P, 26112], f32r)

        def part(at, n, width):
            return arena[:, at:at + n * width].rearrange("p (n t) -> p n t", n=n)
        at = 0
        ql = [part(at + i * 2 * TOK, 2, TOK) for i in range(2)]
        at += 4 * TOK
        kvl = [part(at + i * TOK, 1, TOK) for i in range(2)]
        at += 2 * TOK
        kr = [part(at + i * TOK, 1, TOK) for i in range(2)]
        at += 2 * TOK
        base = at
        h = [part(base + i * HT, DT, TOK) for i in range(2)]
        pd = [part(base + 2 * HT + i * 4 * TOK, 4, TOK) for i in range(2)]
        hid = [[part(base + 2 * HT + (2 * s + i) * 2 * TOK, 2, TOK) for i in range(2)] for s in range(2)]
        mg = h
        at = base
        qn = [part(at + i * 2 * TOK, 2, TOK) for i in range(2)]
        at += 4 * TOK
        qr = [part(at + i * TOK, 1, TOK) for i in range(2)]
        at += 2 * TOK
        kn = [part(at + i * 2 * TOK, 2, TOK) for i in range(2)]
        at += 4 * TOK
        vv = [part(at + i * KT_ALL * 256, KT_ALL, 256) for i in range(2)]
        at += 2 * KT_ALL * 256
        pt = [[part(at + (2 * s + i) * KT_ALL * 256, KT_ALL, 256) for i in range(2)] for s in range(2)]
        at += 4 * KT_ALL * 256
        oo = [part(at + i * 2 * TOK, 2, TOK) for i in range(2)]
        at += 4 * TOK
        assert at <= 26112
        cst = sb("cst", [P, DT * 4 + 124], f32r)
        ada_hi, ada_lo = (arena[:, i * BLK:(i + 1) * BLK] for i in range(2))
        assert 2 * BLK <= base
        big = sb("big", [P, 2 * DT, TOK])
        xs, ys = big[:, 0:DT, :], big[:, DT:2 * DT, :]
        ybuf = ys.rearrange("p n t -> p (n t)")
        u_pad = ybuf[:, 0:NG * U_LEN].rearrange("p (g t) -> p g t", g=NG)
        tmp_all = sb("tmp", [P, 2 * U_LEN + 3 * TOK])
        tmp = [tmp_all[:, i * U_LEN:i * U_LEN + TOK] for i in range(2)]
        tmp += [tmp_all[:, 2 * U_LEN + i * TOK:2 * U_LEN + (i + 1) * TOK] for i in range(3)]
        ptmp = [tmp_all[:, i * U_LEN:(i + 1) * U_LEN] for i in range(2)]
        rope_t = sb("rope_t", [P, 2, SEQ])
        ident = sb("ident", [P, P])
        ones = sb("ones", [P, P])
        edge = sb("edge", [P, NG, 2, 2, PAD])
        pair_sum = sb("pair_sum", [4, 2])
        vecs = sb("vecs", [P, DEPTH, n_vec])
        mods = sb("mods", [P, 48, 2])
        gain = sb("gain", [P, 4, DT, 2])
        csil = sb("csil", [P, 16])
        mrow = sb("mrow", [4, 2, 256])
        small = sb("small", [P, 2, 16])
        zero = sb("zero", [P, 1])
        power = sb("power", [P, TOK // P])
        st = sb("st", [P, 3, 8])
        acc = es.enter_context(nc.psum_tensor("acc", [P, 4 * UNIT], f32))

        def unit(g):
            return acc[:, (g % 4) * UNIT:(g % 4 + 1) * UNIT]

        stage_full = [sem("stage_full0"), sem("stage_full1")]
        whi_ready, wlo_ready = sem("whi_ready"), sem("wlo_ready")
        mm_done, read_a, read_d = sem("mm_done"), sem("read_a"), sem("read_d")
        pair_in = sem("pair_in")
        ident_in, consts_in, x_in, rows_in = sem("ident_in"), sem("consts_in"), sem("x_in"), sem("rows_in")
        cleared, x_saved, x_back, out_sent = sem("cleared"), sem("x_saved"), sem("x_back"), sem("out_sent")
        c_ready, mods_step = sem("c_ready"), sem("mods_step")
        sq_done, sq_added, rstd_done, diag_done = sem("sq_done"), sem("sq_added"), sem("rstd_done"), sem("diag_done")
        n_scaled, n_hi, n_full, n_lo, x_upd = sem("n_scaled"), sem("n_hi"), sem("n_full"), sem("n_lo"), sem("x_upd")
        pool_step, pool_done, pd_hi, pd_lo = sem("pool_step"), sem("pool_done"), sem("pd_hi"), sem("pd_lo")
        wp_hi, swap_hi, swap_lo = sem("wp_hi"), sem("swap_hi"), sem("swap_lo")
        rope_sum, rope_step, rope_hi, rope_lo = sem("rope_sum"), sem("rope_step"), sem("rope_hi"), sem("rope_lo")
        proj_hi, smax, p_norm, pt_hi, o_hi = sem("proj_hi"), sem("smax"), sem("p_norm"), sem("pt_hi"), sem("o_hi")
        merged_add, mg_hi, mg_lo = sem("merged_add"), sem("mg_hi"), sem("mg_lo")
        raw_hi, raw_full = sem("raw_hi"), sem("raw_full")
        ada_hi_ready, ada_lo_ready = sem("ada_hi_ready"), sem("ada_lo_ready")
        total_clear = sem("total_clear")
        silu_done, hid_hi, hid_lo, y_clear = sem("silu_done"), sem("hid_hi"), sem("hid_lo"), sem("y_clear")

        rows = ybuf.rearrange("p (t n) -> p t n", t=KT_ALL)
        vrow = [tmp[0][:, 0:P], tmp[1][:, 0:P]]

        def tokens(l):
            return TOK if l == 0 else SEQ

        def segs(n):
            return [(0, SEQ)] + ([(SEQ, n)] if n > SEQ else [])

        def freed(p, j, i):
            e, n = p.free_at[j - 4] if j >= 4 else p.free_at[j - 4 + p.groups]
            step = p.da if e == "A" else p.dd
            if j < 4:
                n -= step
            return (read_a if e == "A" else read_d), n + i * step

        def two(dst, src, n):
            a = n // 2
            return [(dst[:, 0:a], src[:, 0:a]), (dst[:, a:n], src[:, a:n])]

        def as3(slot, n, w):
            return stage[:, slot, 0:n * w].rearrange("p (n w) -> p n w", n=n)

        def k_major(w, l):
            return w[l].rearrange("(k p) n -> p k n", p=P)

        def load(kind, l, j, slot):
            if kind == "ada":
                return two(as3(slot, DT, 256), k_major(w_ada, l)[:, :, ds(j * 256, 256)], DT)
            if kind == "in":
                return two(as3(slot, DT, 256), k_major(w_in, l)[:, :, ds(j, 256)], DT)
            if kind == "kv":
                return two(as3(slot, DT, 128), k_major(w_in, l)[:, :, ds(OFF_KV, 128)], DT)
            if kind == "kr":
                src = k_major(w_in, l)[:, :, ds(OFF_KR, ROPE)]
                dst = as3(slot, DT, 256)
                return [(dst[:, :, 0:ROPE], src), (dst[:, :, ROPE:2 * ROPE], src)]
            if kind == "pool":
                return two(as3(slot, NG, P), w_pool[l].rearrange("g c e -> c g e"), NG)
            if kind == "o_pool":
                return two(as3(slot, 4, 512), k_major(w_o_pool, l)[:, :, ds(j * 512, 512)], 4)
            if kind == "qk":
                return [(as3(slot, 2, 384), k_major(w_uq, l)[:, :, ds(j * 384, 384)]),
                        (stage[:, slot, 768:1280], w_ukv[l][:, ds(j * 512, 512)])]
            if kind == "o":
                return two(as3(slot, 2, D_MODEL), w_o_mla[l][ds(j * 256, 256), :].rearrange("(k p) n -> p k n", p=P), 2)
            if kind == "out":
                return two(as3(slot, DT, 256), k_major(w_out, l)[:, :, ds(j * 256, 256)], DT)
            if kind == "gate":
                return two(as3(slot, DT, 256), k_major(w_ffn_gate, l)[:, :, ds(j * 256, 256)], DT)
            if kind == "up":
                return two(as3(slot, DT, 256), k_major(w_ffn_up, l)[:, :, ds(j * 256, 256)], DT)
            return two(as3(slot, 2, D_MODEL),
                       w_ffn_down[l][ds(j * 256, 256), :].rearrange("(k p) n -> p k n", p=P), 2)

        def ff_phases(l):
            if l + 1 < DEPTH:
                return [(ph["ff_ada", l], True, 0), (ph["ff", l], False, ADA_TURNS)]
            return [(ph["ff", l], False, 0)]

        def staged(b):
            p = ph["ff_ada", 0]
            if b < p.b:
                return b
            halves, r = divmod(min(b - p.b, p.turns * p.blocks), 3)
            return p.b + 4 * halves + (0, 2, 3)[r] + max(b - p.b - p.turns * p.blocks, 0)

        def stage_of(b):
            return stage[:, staged(b) % 2, :]

        def loads_per_turn(p):
            return staged(p.b + p.blocks) - staged(p.b)

        block = es.enter_context(nc.Block())

        @block.sync
        def _(sp):
            sp.dma_start(ident[:], k_ident).then_inc(ident_in, 16)
            sp.dma_start(pair_sum[:], k_pair).then_inc(pair_in, 16)
            for l in range(DEPTH):
                own = {"b_ada": b_ada, "g_pre_mix": g_pre_mix, "g_post_mix": g_post_mix, "g_pre_ffn": g_pre_ffn,
                       "g_post_ffn": g_post_ffn, "q_norm": q_norm, "kv_norm": kv_norm, "pool_scale": pool_scale}
                for name, (a, b) in vec.items():
                    src = c[0] if name == "c" else c_ctx if name == "c_ctx" else own[name][l]
                    sp.dma_start(vrow[l][a:b, :], src.rearrange("(r q) -> r q", q=P)).then_inc(rows_in, 16)

            def put(kind, l, j, b, p=None, i=0):
                if b >= 2:
                    sp.wait_ge(wlo_ready, b - 1 + i * (p.blocks if p else 0))
                fill(load(kind, l, j, staged(b) % 2), staged(b) % 2)

            def fill(transfers, slot):
                for dst, src in transfers:
                    sp.dma_start(dst, src).then_inc(stage_full[slot], 16)

            for l in range(DEPTH):
                if l == 0:
                    put("ada", 0, 0, 0)
                    put("ada", 0, 1, 1)
                    for t in range(TOK // P):
                        src = x[0, t * P:(t + 1) * P, :] if t < SEQ // P else ctx[0, t * P - SEQ:(t + 1) * P - SEQ, :]
                        sp.dma_start(rows[:, t, :], src).then_inc(x_in, 16)
                    sp.dma_start(rope_t[:], k_rope).then_inc(consts_in, 16)
                    sp.dma_start(edge[:], k_edge).then_inc(consts_in, 16)
                    p = ph["ada", 0]
                    with sp.Fori(0, p.turns) as i:
                        for s in range(2):
                            put("ada", l, 2 * i + (2 + s), p.b + s, p, i)
                p = ph["u", l]
                put("in", l, OFF_POOL, p.b)
                put("in", l, OFF_POOL + 256, p.b + 1)
                p = ph["qkv", l]
                put("in", l, 0, p.b)
                put("kv", l, 0, p.b + 1)
                put("kr", l, 0, p.b + 2)
                for half in range(2):
                    p = ph["g%d" % half, l]
                    with sp.Fori(0, p.turns) as i:
                        for s in range(2):
                            put("in", l, (2 * i + s) * 256 + OFF_GATE + half * D_MODEL, p.b + s, p, i)
                put("pool", l, 0, ph["w_pool", l].b)
                for s in range(2):
                    put("o_pool", l, s, ph["w_o_pool", l].b + s)
                p = ph["pairs", l]
                with sp.Fori(0, p.turns) as i:
                    put("qk", l, i, p.b, p, i)
                    for s in range(4):
                        put("ada", l, 4 * i + (8 + s), p.b + 1 + s, p, i)
                    put("o", l, i, p.b + 5, p, i)
                p = ph["w_out", l]
                with sp.Fori(0, p.turns) as i:
                    for s in range(2):
                        put("out", l, 2 * i + s, p.b + s, p, i)
                p = ph["ff_first", l]
                put("gate", l, 0, p.b)
                put("up", l, 0, p.b + 1)
                for p, with_ada, before in ff_phases(l):
                    with sp.Fori(0, p.turns) as i:
                        for s in range(2):
                            j = 2 * before + s
                            b = p.b + 3 * s
                            put("gate", l, 2 * i + (j + 1), b, p, i)
                            if not with_ada:
                                put("up", l, 2 * i + (j + 1), b + 1, p, i)
                                put("down", l, 2 * i + j, b + 2, p, i)
                                continue
                            slot = 1 - staged(b) % 2
                            sp.wait_ge(wlo_ready, b + i * p.blocks)
                            fill(load("ada", l + 1, 2 * i + s, slot), slot)
                            sp.wait_ge(wlo_ready, b + 1 + i * p.blocks)
                            fill(load("up", l, 2 * i + (j + 1), 1 - slot), 1 - slot)
                            sp.wait_ge(ada_lo_ready, 2 * i + (s + 1))
                            fill(load("down", l, 2 * i + j, slot), slot)
                put("down", l, FF_GROUPS - 1, ph["ff_last", l].b)
            p = ph["out"]
            for t in range(SEQ // P):
                e, n = p.free_at[t]
                sp.wait_ge(read_a if e == "A" else read_d, n)
                sp.dma_start(out[0, t * P:(t + 1) * P, :], rows[:, t, :]).then_inc(out_sent, 16)
            sp.wait_ge(out_sent, 16 * (SEQ // P))

        def after(per_pair, l, i, k):
            return l * PAIRS * per_pair[0] + i * per_pair[l] + k

        N_TILES = [len(attention_tiles(l)) for l in range(DEPTH)]
        N_STAT = [2 * n for n in N_TILES]
        N_PV = [len(pv_sets(l)) for l in range(DEPTH)]
        V_TILES = [[(0, 2), (2, 4), (4, 5), (5, 6)], [(0, 4), (4, 6)]]
        N_PROJ = [4 + len(v) for v in V_TILES]

        def as_values(u, n):
            return u[:, 0:n * 256].rearrange("p (n w) -> p n w", n=n)

        def score_places(l, t, u):
            e = tmp[2 + t % 3]
            if attention_tiles(l)[t][2]:
                return [(u[:, 0:CTX], e[:, 0:CTX]), (u[:, SEQ:SEQ + CTX], e[:, CTX:2 * CTX])]
            return [(u[:, 0:TOK], e[:, 0:TOK])]

        def turned_places(l, t, u):
            _, n, of_ctx = attention_tiles(l)[t]
            k = next(k for k, own in pv_sets(l).values() if t in own)
            if of_ctx:
                return u[:, 0:2 * CTX].rearrange("p (n w) -> p n w", n=2), [pt[k % 2][i][:, 0:2, :] for i in range(2)]
            a = (n % 2) * P
            return (u[:, 0:TOK].rearrange("p (n w) -> p n w", n=KT_ALL),
                    [pt[k % 2][i][:, :, a:a + P] for i in range(2)])

        def pv_place(l, k):
            own = next(own for n, own in pv_sets(l).values() if n == k)
            hd, n, of_ctx = attention_tiles(l)[own[-1]]
            return (hd, SEQ, SEQ // P) if of_ctx else (hd, (n // 2) * 256, 0)

        def swap_places(w, keys, half):
            if keys:
                v = w.rearrange("p (k s a h c) -> p k s a h c", k=DT, s=2, a=4, h=2)
                return v[:, :, 0, :, half, :], v[:, :, 1, :, 1 - half, :]
            q = w[:, 0:768].rearrange("p (k n) -> p k n", k=4)[:, :, NOPE:NOPE + ROPE]
            src = q.rearrange("p k (a h c) -> p k a h c", a=2, h=2)
            dst = w[:, 1536:1792].rearrange("p (k a h c) -> p k a h c", k=4, a=2, h=2)
            return src[:, :, :, half, :], dst[:, :, :, 1 - half, :]

        def rope_places(w):
            return (w[:, 0:768].rearrange("p (k n) -> p k n", k=4)[:, :, NOPE:NOPE + ROPE],
                    w[:, 1280:1536].rearrange("p (k n) -> p k n", k=4))

        def updated(e, key, k):
            n = plan.norms[key]
            if k < n["nk"] - 1:
                e.wait_ge(x_upd, n["upd"] + k + 1)
            else:
                e.wait_ge(read_d, n["at"][1][1])

        def msq(key):
            return small[:, int(key[0] == "kv"), 0:plan.norms[key]["T"] // P]

        def latent(r, T):
            return [(ql[i][:, r, 0:T] if r < 2 else kvl[i][:, 0, :]) for i in range(2)]

        def rstd(key):
            return small[:, int(key[0] == "kv"), 8:8 + plan.norms[key]["T"] // P]

        def shared(key):
            return key[0] in ("pre_mix", "pre_ffn") and key != ("pre_mix", 0)

        def slots_of(key):
            return {"q": (3, 2, 4), "kv": (3, 3, 3)}.get(key[0], (0, 2, 3))

        def x_ready(e, key, k):
            what, l = key
            if what == "pre_ffn":
                updated(e, ("post_mix", l), k)
            elif l:
                updated(e, ("post_ffn", l - 1), k)
            else:
                e.wait_ge(read_a, ph["x_in"].free_at[k][1])

        def scale_of(key, k, v):
            what, l = key
            if what == "q":
                return vecs[:, l, vec["q_norm"][0] + k:vec["q_norm"][0] + k + 1]
            if what == "kv":
                return vecs[:, l, vec["kv_norm"][0]:vec["kv_norm"][0] + 1]
            n = {"pre_mix": 0, "post_mix": 1, "pre_ffn": 2, "post_ffn": 3}[what]
            return gain[:, n, k, v:v + 1]

        def shift_of(key, k, v):
            if key[0] in ("q", "kv"):
                return zero[:]
            m = {"pre_mix": DT, "pre_ffn": 4 * DT}[key[0]]
            return mods[:, m + k, v:v + 1]

        def steps_of_pool(l, g):
            streams = 2 if l == 0 else 1
            per = [n + 1 + 2 * streams + 2 for n in range(NG)]
            before = 0 if l == 0 else 3 + sum(n + 1 + 4 + 2 for n in range(NG))
            return before + 3 + sum(per[:g + 1])

        @block.gpsimd
        def _(pool):
            nc.gpsimd.memset(ones[:], 1.0).then_inc(cleared, 1)
            nc.gpsimd.memset(zero[:], 0.0).then_inc(cleared, 1)
            nc.gpsimd.memset(cst[:].bitcast(f32), 0.0).then_inc(cleared, 1)
            nc.gpsimd.memset(power[:], -0.5).then_inc(cleared, 1)
            nc.gpsimd.memset(tmp[2][:], 0.0).then_inc(total_clear, 1)
            pool.wait_ge(cleared, 4)

            def inverse(key):
                pool.wait_ge(read_d, plan.norms[key]["at"][0][1])
                nc.gpsimd.tensor_tensor(rstd(key), msq(key), power[:, 0:plan.norms[key]["T"] // P], ALU.pow
                                        ).then_inc(rstd_done, 1)

            def norm(key):
                n, T = plan.norms[key], plan.norms[key]["T"]
                if shared(key):
                    for k in range(1, n["nk"] - 1):
                        pool.wait_ge(sq_done, n["sq"] + k + 1)
                        if k > 1:
                            pool.wait_ge(sq_added, n["adds"] + k - 1)
                        nc.gpsimd.tensor_tensor(tmp[2][:, 0:T], (tmp[0] if k == 1 else tmp[2])[:, 0:T],
                                                tmp[k % 2][:, 0:T], ALU.add).then_inc(sq_added, 1)
                if key[0] not in ("q", "kv"):
                    inverse(key)
                if key[0].startswith("post"):
                    return
                for k in range(n["nk"]):
                    pool.wait_ge(n_scaled, n["sq"] + k + 1)
                    for v, (a, b) in enumerate(segs(T)):
                        last = nc.gpsimd.tensor_scalar(tmp[3 + k % 2][:, a:b], tmp[k % 2][:, a:b],
                                                       scale_of(key, k, v), shift_of(key, k, v), ALU.mult, ALU.add)
                    last.then_inc(n_full, 1)

            def clear_total(l):
                pool.wait_ge(rope_lo, (l + 1) * (PAIRS + 1))
                nc.gpsimd.memset(tmp[2][:, 0:tokens(l)], 0.0).then_inc(total_clear, 1)

            for l in range(DEPTH):
                norm(("pre_mix", l))
                n = (l > 0) * steps_of_pool(0, NG - 1)
                for a, b in ((0, U_X), (U_X + SEQ, U_C), (U_C + CTX, U_LEN)):
                    nc.gpsimd.memset(u_pad[:, :, a:b], 0.0).then_inc(pool_step, 1)
                n += 3
                pool.wait_ge(read_a, ph["u", l].free_at[-1][1])
                a, b = U_X, (U_C + CTX if l == 0 else U_X + SEQ)
                for g, w in enumerate(WINDOWS):
                    src, m = u_pad[:, g, :], 1
                    for level in range(g + 1):
                        dst, cols = ptmp[level % 2], b + PAD - 2 * m + 1
                        pool.wait_ge(pool_step, n)
                        nc.gpsimd.tensor_tensor(dst[:, 0:cols], src[:, 0:cols], src[:, m:m + cols], ALU.add
                                                ).then_inc(pool_step, 1)
                        src, m, n = dst, 2 * m, n + 1
                    half = w // 2
                    for side, at in ((0, U_X), (1, U_X + SEQ - PAD)):
                        for t in range(2 if l == 0 else 1):
                            at_t = at + t * (U_C - U_X if side == 0 else U_C + CTX - U_X - SEQ) - half
                            pool.wait_ge(pool_step, n)
                            nc.gpsimd.tensor_tensor(src[:, at_t:at_t + PAD], src[:, at_t:at_t + PAD],
                                                    edge[:, g, side, t, :], ALU.mult).then_inc(pool_step, 1)
                            n += 1
                    pool.wait_ge(pool_step, n)
                    nc.gpsimd.tensor_scalar(src[:, a - half:b - half], src[:, a - half:b - half], 1.0 / w, 0.0,
                                            ALU.mult, ALU.add).then_inc(pool_step, 1)
                    pool.wait_ge(pool_step, n + 1)
                    nc.gpsimd.tensor_tensor(u_pad[:, g, a:b], src[:, a - half:b - half], u_pad[:, g, a:b],
                                            ALU.subtract).then_inc(pool_step, 1)
                    n += 2
                    assert n == steps_of_pool(l, g)
                for key in (("q", l), ("kv", l)):
                    inverse(key)
                for key in (("q", l), ("kv", l)):
                    norm(key)
                p = ph["pairs", l]
                with pool.Fori(0, p.turns) as i:
                    pool.wait_ge(wlo_ready, p.b + 1 + i * p.blocks)
                    block_lo = w_lo[:, p.b % 2, :]
                    for k in (0, 2):
                        nc.gpsimd.tensor_tensor(rope_places(block_lo)[1][:, k:k + 2],
                                                rope_places(block_lo.bitcast(f32))[0][:, k:k + 2],
                                                ones[:].rearrange("p (k n) -> p k n", k=2), ALU.mult)
                    for half in range(2):
                        last = nc.gpsimd.tensor_tensor(swap_places(block_lo, False, half)[1],
                                                       swap_places(block_lo.bitcast(f32), False, half)[0],
                                                       ones[:].rearrange("p (k a c) -> p k a c", k=4, a=2), ALU.mult)
                    last.then_inc(swap_lo, 1)
                    for s in (1, 2, 3, 4, 6):
                        pool.wait_ge(wlo_ready, p.b + s + i * p.blocks)
                        pool.wait_ge(whi_ready, p.b + s + 1 + i * p.blocks)
                        slot = (p.b + s) % 2
                        nc.gpsimd.tensor_tensor(w_lo[:, slot, :], stage_of(p.b + s), w_hi[:, slot, :].bitcast(f32),
                                                ALU.subtract).then_inc(wlo_ready, 1)
                clear_total(l)
                for key in (("post_mix", l), ("pre_ffn", l)):
                    norm(key)
                clear_total(l)
                nc.gpsimd.memset(ys, 0.0).then_inc(y_clear, 1)
                if l + 1 < DEPTH:
                    with pool.Fori(0, ADA_TURNS) as i:
                        for s in range(2):
                            pool.wait_ge(ada_hi_ready, 2 * i + (s + 1))
                            raw_block = stage[:, 1 - staged(ph["ff_ada", l].b + 3 * s) % 2, :]
                            nc.gpsimd.tensor_tensor(ada_lo, raw_block, ada_hi.bitcast(f32), ALU.subtract
                                                    ).then_inc(ada_lo_ready, 1)
                norm(("post_ffn", l))

        @block.scalar
        def _(act):
            def split(b, p, i=0):
                act.wait_ge(stage_full[staged(b) % 2], 32 * (staged(b) // 2 + 1) + i * (16 * loads_per_turn(p)))
                if b >= 2:
                    act.wait_ge(mm_done, (p.g if b - 2 < p.b and p.turns > 1 else plan.end[b - 2]) + i * p.groups)
                nc.scalar.activation(w_hi[:, b % 2, :], stage_of(b), ACT.Copy).then_inc(whi_ready, 1)

            def copy_out(p, j, dst, n, i=0, func=ACT.Copy):
                act.wait_ge(mm_done, p.g + j + 1 + i * p.groups)
                nc.scalar.activation(dst, unit(p.g + j)[:, 0:n], func).then_inc(read_a, 1)

            def swap(b, p, keys, i=0):
                act.wait_ge(wlo_ready, b + 1 + i * p.blocks)
                if not keys:
                    nc.scalar.activation(rope_places(w_hi[:, b % 2, :])[1],
                                         rope_places(w_hi[:, b % 2, :].bitcast(f32))[0], ACT.Copy)
                for half in range(2):
                    src, _ = swap_places(w_hi[:, b % 2, :].bitcast(f32), keys, half)
                    _, dst = swap_places(w_hi[:, b % 2, :], keys, half)
                    last = nc.scalar.activation(dst, src, ACT.Copy) if half == 0 else \
                        nc.scalar.activation(dst, src, ACT.Copy).then_inc(swap_hi, 1)

            def squares(key, src, ready):
                n = plan.norms[key]
                if n["full"]:
                    act.wait_ge(n_full, n["full"])
                    act.wait_ge(n_hi, n["full"])
                for k in range(n["nk"]):
                    ready(k)
                    if k >= 2:
                        act.wait_ge(sq_added, n["adds"] + (max(k - 2, 1) if shared(key) else k - 1))
                    nc.scalar.activation(tmp[slots_of(key)[0] + k % 2][:, 0:n["T"]], src[:, k, 0:n["T"]], ACT.Square
                                         ).then_inc(sq_done, 1)

            def norm_hi(key, hi):
                n = plan.norms[key]
                for k in range(n["nk"]):
                    act.wait_ge(n_scaled, n["sq"] + k + 1)
                    for v, (a, b) in enumerate(segs(n["T"])):
                        last = nc.scalar.activation(hi[:, k, a:b], tmp[k % 2][:, a:b], ACT.Identity,
                                                    bias=shift_of(key, k, v), scale=scale_of(key, k, v))
                    last.then_inc(n_hi, 1)

            def ada_rows(p, j, s, i):
                act.wait_ge(mm_done, p.g + j + 1 + i * p.groups)
                nc.scalar.activation(mrow[:, s % 2, :], unit(p.g + j)[0:4, 0:256], ACT.Copy).then_inc(read_a, 1)

            split(0, ph["ada", 0])
            act.wait_ge(read_d, ph["vectors"].free_at[0][1])
            a = vec["c"][0]
            nc.scalar.activation(csil[:], vecs[:, 0, a:a + 2 * DT], ACT.Silu).then_inc(c_ready, 1)
            act.wait_ge(c_ready, 1)
            act.wait_ge(cleared, 4)
            for v in range(2):
                nc.scalar.activation(cst[:, 0:DT * 4].rearrange("p (k f) -> p k f", f=4)[:, :, 2 * v],
                                     csil[:, v * DT:(v + 1) * DT], ACT.Copy).then_inc(c_ready, 1)
            split(1, ph["ada_first", 0])
            for s in range(2):
                ada_rows(ph["ada_first", 0], s, s, 0)
            for k in range(DT):
                act.wait_ge(mm_done, ph["x_in"].g + k + 1)
                if k >= 2:
                    act.wait_ge(sq_added, k - 1)
                nc.scalar.activation(tmp[k % 2][:, 0:TOK], unit(ph["x_in"].g + k)[:, 0:TOK], ACT.Square
                                     ).then_inc(sq_done, 1)
                copy_out(ph["x_in"], k, xs[:, k, :], TOK)
                if k % 4 == 3:
                    split(2 + k // 4, ph["ada_first", 0])
            for l in range(DEPTH):
                T = tokens(l)
                key = ("pre_mix", l)
                if l == 0:
                    p = ph["ada", l]
                    with act.Fori(0, p.turns) as i:
                        for s in range(2):
                            ada_rows(p, s, s, i)
                            split(p.b + s + 2, p, i)
                else:
                    squares(key, xs, lambda k: x_ready(act, key, k))
                act.dma_start(x_keep[:, :, 0:T], xs[:, :, 0:T]).then_inc(x_saved, 16)
                if l:
                    split(ph["u", l].b + 1, ph["u", l])
                norm_hi(key, h[0])
                p = ph["u", l]
                for s in range(2):
                    if s:
                        split(p.b + s + 1, p)
                    for j in (2 * s, 2 * s + 1):
                        act.wait_ge(mm_done, p.g + j + 1)
                        if l == 0:
                            nc.scalar.activation(u_pad[:, j, U_C:U_C + CTX], unit(p.g + j)[:, SEQ:TOK], ACT.Copy)
                        nc.scalar.activation(u_pad[:, j, U_X:U_X + SEQ], unit(p.g + j)[:, 0:SEQ], ACT.Copy
                                             ).then_inc(read_a, 1)
                p = ph["qkv", l]
                split(p.b + 1, p)
                for r in range(3):
                    if r == 2:
                        split(p.b + 2, p)
                    act.wait_ge(mm_done, p.g + r + 1)
                    nc.scalar.activation(latent(r, T)[0], unit(p.g + r)[:, 0:T if r < 2 else TOK], ACT.Copy
                                         ).then_inc(raw_hi, 1)
                swap(p.b + 2, p, True)
                split(p.b + 3, p)
                act.wait_ge(rope_sum, 1 + l * (PAIRS + 1))
                nc.scalar.activation(kr[0][:, 0, :], tmp[2][:, :], ACT.Copy).then_inc(rope_hi, 1)
                for r in range(3):
                    act.wait_ge(raw_full, 6 * l + r + 1)
                    rows_of = tmp[3 + r % 2][:, 0:T if r < 2 else TOK]
                    nc.scalar.activation(rows_of, rows_of, ACT.Square).then_inc(sq_done, 1)
                for half in range(2):
                    p = ph["g%d" % half, l]
                    if half == 0:
                        act.wait_ge(x_saved, 16 * (l + 1))
                    else:
                        for g in range(NG):
                            act.wait_ge(pool_step, steps_of_pool(l, g))
                            for v, (a, b) in enumerate(segs(T)):
                                off = U_C - SEQ if v else U_X
                                last = nc.scalar.activation(pd[0][:, g, a:b], u_pad[:, g, a + off:b + off], ACT.Copy)
                            last.then_inc(pd_hi, 1)
                        act.wait_ge(pd_lo, NG * (l + 1))
                    with act.Fori(0, p.turns) as i:
                        for s in range(2):
                            split(p.b + s + 1, p, i)
                            for j in (2 * s, 2 * s + 1):
                                copy_out(p, j, big[:, ds(4 * i + (half * DT + j), 1), 0:T], T, i, ACT.Sigmoid)
                p = ph["w_pool", l]
                split(p.b + 1, p)
                a = vec["pool_scale"][0]
                for g in range(NG):
                    act.wait_ge(mm_done, p.g + g + 1)
                    nc.scalar.activation(pd[0][:, g, 0:T], unit(p.g + g)[:, 0:T], ACT.Copy,
                                         scale=vecs[:, l, a + g:a + g + 1]).then_inc(wp_hi, 1)
                p = ph["w_o_pool", l]
                split(p.b + 1, p)
                split(p.b + 2, p)
                norm_hi(("q", l), ql[0])
                norm_hi(("kv", l), kvl[0])
                p = ph["pairs", l]
                with act.Fori(0, p.turns) as i:
                    def parts(j, dst, src, scale=1.0):
                        act.wait_ge(mm_done, p.g + j + 1 + i * p.groups)
                        nc.scalar.activation(dst, src, ACT.Copy, scale=scale).then_inc(proj_hi, 1)
                    swap(p.b, p, False, i)
                    split(p.b + 1, p, i)
                    for hd in range(2):
                        parts(hd, qn[0][:, hd, 0:T], unit(p.g + hd)[:, 0:T], SCALE)
                    for hd in range(2):
                        parts(2 + hd, kn[0][:, hd, :], unit(p.g + 2 + hd)[:, 0:TOK])
                    for j, (a, b) in enumerate(V_TILES[l]):
                        parts(6 + j, vv[0][:, a:b, :], as_values(unit(p.g + 6 + j), b - a))
                    act.wait_ge(rope_sum, 2 + l * (PAIRS + 1) + i)
                    nc.scalar.activation(qr[0][:, 0, 0:T], tmp[2][:, 0:T], ACT.Copy, scale=SCALE).then_inc(rope_hi, 1)
                    j0 = 6 + len(V_TILES[l])
                    for kind, t in attention_order(l):
                        if kind == "H":
                            split(p.b + t, p, i)
                        if kind in "HLC":
                            continue
                        j = j0 + attention_groups(l).index((kind, t))
                        u = unit(p.g + j)
                        if kind == "R":
                            ada_rows(p, j, t, i)
                            continue
                        act.wait_ge(mm_done, p.g + j + 1 + i * p.groups)
                        if kind == "S":
                            act.wait_ge(smax, after(N_TILES, l, i, t + 1))
                            for v, (src, dst) in enumerate(score_places(l, t, u)):
                                last = nc.scalar.activation(dst, src, ACT.Exp, bias=st[:, t % 3, v:v + 1],
                                                            accum_out=st[:, t % 3, 4 + v:5 + v])
                            last.then_inc(read_a, 1)
                        elif kind == "T":
                            src, dst = turned_places(l, t, u)
                            nc.scalar.activation(dst[0], src, ACT.Copy).then_inc(pt_hi, 1)
                        else:
                            hd, a, _ = pv_place(l, t)
                            nc.scalar.activation(oo[0][:, hd, a:a + 256], u[:, 0:256], ACT.Copy).then_inc(o_hi, 1)
                for k in range(DT):
                    act.wait_ge(merged_add, (l + 1) * PAIRS * DT - DT + k + 1)
                    nc.scalar.activation(mg[0][:, k, 0:T], ys[:, k, 0:T], ACT.Copy).then_inc(mg_hi, 1)
                act.dma_start(xs[:, :, 0:T], x_keep[:, :, 0:T]).then_inc(x_back, 16)
                act.wait_ge(mg_lo, (l + 1) * DT)
                p = ph["w_out", l]
                adds = plan.norms["post_mix", l]["adds"]
                with act.Fori(0, p.turns) as i:
                    for s in range(2):
                        split(p.b + s + 1, p, i)
                        for j in (2 * s, 2 * s + 1):
                            act.wait_ge(mm_done, p.g + j + 1 + i * p.groups)
                            act.wait_ge(sq_added, adds + j - 1 + i * p.groups)
                            nc.scalar.activation(tmp[j % 2][:, 0:T], unit(p.g + j)[:, 0:T], ACT.Square
                                                 ).then_inc(sq_done, 1)
                            copy_out(p, j, ys[:, ds(4 * i + j, 1), 0:T], T, i)
                split(ph["ff_first", l].b + 1, ph["ff_first", l])
                squares(("pre_ffn", l), xs, lambda k: x_ready(act, ("pre_ffn", l), k))
                norm_hi(("pre_ffn", l), h[0])

                def hidden(p, j, n, i=0):
                    for m in range(2):
                        act.wait_ge(mm_done, p.g + j + m + 1 + i * p.groups)
                        nc.scalar.activation(tmp[m][:, 0:T], unit(p.g + j + m)[:, 0:T], ACT.Silu
                                             ).then_inc(silu_done, 1)

                def hidden_hi(p, j, s, i=0):
                    for m in range(2):
                        act.wait_ge(read_d, p.free_at[j + m][1] + i * p.dd)
                        nc.scalar.activation(hid[s][0][:, m, 0:T], tmp[3 + m][:, 0:T], ACT.Copy).then_inc(hid_hi, 1)

                p = ph["ff_first", l]
                hidden(p, 0, 0)
                split(p.b + 2, p)
                hidden_hi(p, 2, 0)
                for p, with_ada, _ in ff_phases(l):
                    with act.Fori(0, p.turns) as i:
                        for s in range(2):
                            j = p.groups // 2 * s
                            if with_ada:
                                at = staged(p.b + 3 * s) + 1
                                act.wait_ge(stage_full[at % 2], 32 * (at // 2 + 1) + i * (16 * loads_per_turn(p)))
                                act.wait_ge(mm_done, p.g + j + 5 - p.groups // 2 + i * p.groups)
                                nc.scalar.activation(ada_hi, stage[:, at % 2, :], ACT.Copy).then_inc(ada_hi_ready, 1)
                            split(p.b + 3 * s + 1, p, i)
                            hidden(p, j, 0, i)
                            split(p.b + 3 * s + 2, p, i)
                            hidden_hi(p, j + 2, 1 - s, i)
                            if with_ada:
                                ada_rows(p, j + 4, s, i)
                            split(p.b + 3 * s + 3, p, i)
                p = ph["ff_last", l]
                if l + 1 < DEPTH:
                    split(p.b + 1, p)
                squares(("post_ffn", l), ys, lambda k: act.wait_ge(read_d, p.rd + k + 1))
            p = ph["out"]
            for t in (0, 2):
                copy_out(p, t, rows[:, t, :], D_MODEL)

        @block.vector
        def _(dve):
            def split(b, p, i=0):
                dve.wait_ge(whi_ready, b + 1 + i * p.blocks)
                nc.vector.tensor_tensor(w_lo[:, b % 2, :], stage_of(b), w_hi[:, b % 2, :].bitcast(f32),
                                        ALU.subtract).then_inc(wlo_ready, 1)

            def swap(b):
                dve.wait_ge(wlo_ready, b + 1)
                for half in range(2):
                    src, _ = swap_places(w_lo[:, b % 2, :].bitcast(f32), True, half)
                    _, dst = swap_places(w_lo[:, b % 2, :], True, half)
                    last = nc.vector.tensor_copy(dst, src)
                last.then_inc(swap_lo, 1)

            def minus_hi(dst, full, hi):
                return nc.vector.tensor_tensor(dst, full, hi.bitcast(f32), ALU.subtract)

            def add_squares(key):
                n, (first, total, _) = plan.norms[key], slots_of(key)
                T = n["T"]
                for k in range(1, n["nk"]):
                    dve.wait_ge(sq_done, n["sq"] + k + 1)
                    if k > 1:
                        dve.wait_ge(sq_added, n["adds"] + k - 1)
                    nc.vector.tensor_tensor(tmp[total][:, 0:T], tmp[first if k == 1 else total][:, 0:T],
                                            tmp[first + k % 2][:, 0:T], ALU.add).then_inc(sq_added, 1)

            def add_row(key, k, i=0, turn=0):
                n = plan.norms[key]
                T = n["T"]
                dve.wait_ge(sq_done, n["sq"] + k + 1 + i * turn)
                dve.wait_ge(sq_added, n["adds"] + k + i * turn)
                nc.vector.tensor_tensor(tmp[2][:, 0:T], tmp[2][:, 0:T], tmp[k % 2][:, 0:T], ALU.add
                                        ).then_inc(sq_added, 1)

            def mean_squares(key):
                g, T = plan.norms[key]["at"][0][0], plan.norms[key]["T"]
                dve.wait_ge(mm_done, g + 1)
                nc.vector.tensor_scalar(msq(key), unit(g)[:, 0:T // P],
                                        1.0 / {"q": Q_LORA, "kv": KV_LORA}.get(key[0], D_MODEL), EPS,
                                        ALU.mult, ALU.add).then_inc(read_d, 1)

            def diagonal(key):
                n = plan.norms[key]
                dve.wait_ge(rstd_done, n["n"] + 1)
                for t in range(n["T"] // P):
                    last = nc.vector.tensor_scalar(tmp[slots_of(key)[2]][:, t * P:(t + 1) * P], ident[:],
                                                   rstd(key)[:, t:t + 1], None, ALU.mult)
                last.then_inc(diag_done, 1)

            def stats(key, meanwhile=None):
                if shared(key):
                    n = plan.norms[key]
                    k, T = n["nk"] - 1, n["T"]
                    dve.wait_ge(sq_done, n["sq"] + k + 1)
                    dve.wait_ge(sq_added, n["adds"] + k - 1)
                    nc.vector.tensor_tensor(tmp[2][:, 0:T], tmp[2][:, 0:T], tmp[k % 2][:, 0:T], ALU.add
                                            ).then_inc(sq_added, 1)
                mean_squares(key)
                if meanwhile:
                    meanwhile()
                diagonal(key)
                spread(key)

            def scaled(key, src, k, slot=0):
                n = plan.norms[key]
                if src is None:
                    r = k + 2 * (key[0] == "kv")
                    restore(key[1], r, tmp[k % 2])
                    dve.wait_ge(raw_full, 6 * key[1] + 3 + r + 1)
                    nc.vector.tensor_tensor(tmp[k % 2][:, 0:n["T"]], tmp[k % 2][:, 0:n["T"]],
                                            unit(n["at"][1][0])[:, 0:n["T"]], ALU.mult).then_inc(n_scaled, 1)
                    return
                nc.vector.tensor_tensor(tmp[slot + k % 2][:, 0:n["T"]], src[:, k, 0:n["T"]],
                                        unit(n["at"][1][0])[:, 0:n["T"]], ALU.mult).then_inc(n_scaled, 1)

            def restore(l, r, dst):
                hi, lo = latent(r, tokens(l))
                nc.vector.tensor_tensor(dst[:, 0:tokens(l) if r < 2 else TOK], hi.bitcast(f32), lo.bitcast(f32), ALU.add
                                        ).then_inc(raw_full, 1)

            def spread(key):
                dve.wait_ge(mm_done, plan.norms[key]["at"][1][0] + 1)

            def norm(key, src, lo, hi):
                n = plan.norms[key]
                scaled(key, src, 0)
                for k in range(n["nk"]):
                    if k + 1 < n["nk"]:
                        scaled(key, src, k + 1)
                    dve.wait_ge(n_hi, n["full"] + k + 1)
                    dve.wait_ge(n_full, n["full"] + k + 1)
                    minus_hi(lo[:, k, 0:n["T"]], tmp[3 + k % 2][:, 0:n["T"]], hi[:, k, 0:n["T"]]
                             ).then_inc(n_lo if k + 1 < n["nk"] else read_d, 1)

            def residual(key, meanwhile=None):
                n = plan.norms[key]
                stats(key, meanwhile)
                scaled(key, ys, 0, 3)
                for k in range(n["nk"]):
                    if k + 1 < n["nk"]:
                        if k:
                            dve.wait_ge(x_upd, n["upd"] + k)
                        scaled(key, ys, k + 1, 3)
                    dve.wait_ge(n_scaled, n["sq"] + k + 1)
                    for v, (a, b) in enumerate(segs(n["T"])):
                        last = nc.vector.scalar_tensor_tensor(xs[:, k, a:b], tmp[3 + k % 2][:, a:b], scale_of(key, k, v),
                                                              xs[:, k, a:b], ALU.mult, ALU.add)
                    last.then_inc(x_upd if k + 1 < n["nk"] else read_d, 1)

            def ada_columns(l, p, j, m, i):
                dve.wait_ge(mm_done, p.g + j + 1 + i * p.groups)
                u = unit(p.g + j)[:, 0:4].rearrange("p (m v) -> p m v", v=2)
                for v in range(2):
                    last = nc.vector.tensor_tensor(mods[:, ds(m, 2), v], u[:, :, v], vecs[:, l, ds(m, 2)], ALU.add)
                last.then_inc(read_d, 1)

            def gains(l, which):
                for n in which:
                    name, m, plus = (("g_pre_mix", 0, 1.0), ("g_post_mix", 2 * DT, 0.0), ("g_pre_ffn", 3 * DT, 1.0),
                                     ("g_post_ffn", 5 * DT, 0.0))[n]
                    g = vecs[:, l, vec[name][0]:vec[name][1]]
                    for v in range(2):
                        last = nc.vector.scalar_tensor_tensor(gain[:, n, :, v], mods[:, m:m + DT, v], plus, g,
                                                              ALU.add, ALU.mult)
                last.then_inc(mods_step, 1)

            def rotate(cos_j, p, T, i=0):
                u, w = unit(p.g + cos_j), unit(p.g + cos_j + 1)
                dve.wait_ge(mm_done, p.g + cos_j + 1 + i * p.groups)
                last = nc.vector.tensor_tensor(tmp[3][:, 0:SEQ], u[:, 0:SEQ], rope_t[:, 0, :], ALU.mult)
                if T > SEQ:
                    last = nc.vector.tensor_copy(tmp[2][:, SEQ:TOK], u[:, SEQ:TOK])
                last.then_inc(read_d, 1)
                dve.wait_ge(mm_done, p.g + cos_j + 2 + i * p.groups)
                nc.vector.tensor_tensor(tmp[4][:, 0:SEQ], w[:, 0:SEQ], rope_t[:, 1, :], ALU.mult).then_inc(read_d, 1)
                dve.wait_ge(read_d, p.free_at[cos_j + 1][1] + i * p.dd)
                nc.vector.tensor_tensor(tmp[2][:, 0:SEQ], tmp[3][:, 0:SEQ], tmp[4][:, 0:SEQ], ALU.add
                                        ).then_inc(rope_sum, 1)

            for l in range(DEPTH):
                dve.wait_ge(mm_done, l + 1)
                nc.vector.tensor_copy(vecs[:, l, :], unit(l)[:, 0:n_vec]).then_inc(read_d, 1)
            split(0, ph["ada", 0])
            dve.wait_ge(c_ready, 3)
            for v in range(2):
                cols = cst[:, 0:DT * 4].rearrange("p (k f) -> p k f", f=4)
                last = minus_hi(cols[:, :, 2 * v + 1], csil[:, v * DT:(v + 1) * DT], cols[:, :, 2 * v])
            last.then_inc(c_ready, 1)
            dve.wait_ge(ident_in, 16)
            dve.wait_ge(total_clear, 1)
            p = ph["ada_first", 0]
            split(1, p)
            for s in range(2):
                ada_columns(0, p, 2 + s, 2 * s, 0)
            for k in range(DT):
                add_row(("pre_mix", 0), k)
                if k % 4 == 3:
                    split(2 + k // 4, p)
            dve.wait_ge(consts_in, 32)
            for l in range(DEPTH):
                T = tokens(l)
                if l == 0:
                    mean_squares(("pre_mix", l))
                    diagonal(("pre_mix", l))
                    p = ph["ada", l]
                    with dve.Fori(0, p.turns) as i:
                        for s in range(2):
                            split(p.b + s + 2, p, i)
                        for s in range(2):
                            ada_columns(l, p, 2 + s, 4 * i + (4 + 2 * s), i)
                    dve.wait_ge(read_d, p.rd + p.turns * p.dd)
                    gains(l, (0,))
                dve.wait_ge(mods_step, 2 * l + 1)
                p = ph["u", l]
                if l:
                    stats(("pre_mix", l), lambda: split(p.b + 1, p))
                else:
                    spread(("pre_mix", l))
                norm(("pre_mix", l), xs, h[1], h[0])
                split(p.b + 2, p)
                p = ph["qkv", l]
                split(p.b + 1, p)
                for r in range(3):
                    if r == 2:
                        split(p.b + 2, p)
                    hi, lo = latent(r, T)
                    dve.wait_ge(raw_hi, 3 * l + r + 1)
                    minus_hi(lo, unit(p.g + r)[:, 0:T if r < 2 else TOK], hi).then_inc(read_d, 1)
                swap(p.b + 2)
                split(p.b + 3, p)
                rotate(3, p, TOK)
                dve.wait_ge(rope_hi, 1 + l * (PAIRS + 1))
                minus_hi(kr[1][:, 0, :], tmp[2][:, :], kr[0][:, 0, :]).then_inc(rope_lo, 1)
                dve.wait_ge(rope_lo, 1 + l * (PAIRS + 1))
                dve.wait_ge(read_d, ph["qkv", l].free_at[2][1])
                restore(l, 0, tmp[3])
                restore(l, 1, tmp[4])
                add_squares(("q", l))
                dve.wait_ge(sq_added, plan.norms["kv", l]["adds"])
                restore(l, 2, tmp[3])
                for half in range(2):
                    p = ph["g%d" % half, l]
                    if half == 1:
                        mean_squares(("q", l))
                        mean_squares(("kv", l))
                        for g in range(NG):
                            dve.wait_ge(pd_hi, NG * l + g + 1)
                            for v, (a, b) in enumerate(segs(T)):
                                off = U_C - SEQ if v else U_X
                                last = minus_hi(pd[1][:, g, a:b], u_pad[:, g, a + off:b + off], pd[0][:, g, a:b])
                            last.then_inc(pd_lo, 1)
                        diagonal(("q", l))
                        diagonal(("kv", l))
                    with dve.Fori(0, p.turns) as i:
                        for s in range(2):
                            split(p.b + s + 1, p, i)
                p = ph["w_pool", l]
                split(p.b + 1, p)
                a = vec["pool_scale"][0]
                for g in range(NG):
                    dve.wait_ge(wp_hi, NG * l + g + 1)
                    nc.vector.scalar_tensor_tensor(pd[1][:, g, 0:T], unit(p.g + g)[:, 0:T],
                                                   vecs[:, l, a + g:a + g + 1], pd[0][:, g, 0:T].bitcast(f32),
                                                   ALU.mult, ALU.subtract).then_inc(read_d, 1)
                p = ph["w_o_pool", l]
                for s in range(2):
                    if s == 1:
                        spread(("kv", l))
                        norm(("q", l), None, ql[1], ql[0])
                        norm(("kv", l), None, kvl[1], kvl[0])
                    split(p.b + s + 1, p)
                    for m in range(4):
                        j = 6 * s + m
                        dve.wait_ge(mm_done, p.g + j + 1)
                        nc.vector.tensor_tensor(ys[:, 4 * s + m, 0:T], unit(p.g + j)[:, 0:T], ys[:, 4 * s + m, 0:T],
                                                ALU.mult).then_inc(read_d, 1)
                p = ph["pairs", l]
                groups = attention_groups(l)
                with dve.Fori(0, p.turns) as i:
                    def scaled_lo(dst, src, hi):
                        return nc.vector.scalar_tensor_tensor(dst, src, SCALE, hi.bitcast(f32), ALU.mult, ALU.subtract)

                    def lo_of(j, n, dst, src, hi):
                        dve.wait_ge(proj_hi, after(N_PROJ, l, i, n))
                        minus_hi(dst, src, hi).then_inc(read_d, 1)
                    for hd in range(2):
                        dve.wait_ge(proj_hi, after(N_PROJ, l, i, hd + 1))
                        scaled_lo(qn[1][:, hd, 0:T], unit(p.g + hd)[:, 0:T], qn[0][:, hd, 0:T]).then_inc(read_d, 1)
                    for hd in range(2):
                        lo_of(2 + hd, 3 + hd, kn[1][:, hd, :], unit(p.g + 2 + hd)[:, 0:TOK], kn[0][:, hd, :])
                    rotate(4, p, T, i)
                    for j, (a, b) in enumerate(V_TILES[l]):
                        lo_of(6 + j, 5 + j, vv[1][:, a:b, :], as_values(unit(p.g + 6 + j), b - a), vv[0][:, a:b, :])
                    dve.wait_ge(rope_hi, 2 + l * (PAIRS + 1) + i)
                    scaled_lo(qr[1][:, 0, 0:T], tmp[2][:, 0:T], qr[0][:, 0, 0:T]).then_inc(rope_lo, 1)
                    j0 = 6 + len(V_TILES[l])

                    def probabilities(t):
                        dve.wait_ge(read_a, p.free_at[j0 + groups.index(("S", t))][1] + i * p.da)
                        places = score_places(l, t, unit(0))
                        w = len(places)
                        nc.vector.reciprocal(st[:, t % 3, 6:6 + w], st[:, t % 3, 4:4 + w]).then_inc(p_norm, 1)
                        dve.wait_ge(p_norm, after(N_STAT, l, i, 2 * t + 1))
                        for v, (_, e) in enumerate(places):
                            last = nc.vector.tensor_scalar(e, e, st[:, t % 3, 6 + v:7 + v], None, ALU.mult)
                        last.then_inc(p_norm, 1)

                    for kind, t in attention_order(l):
                        if kind == "L":
                            dve.wait_ge(wlo_ready, p.b + t + i * p.blocks)
                            split(p.b + t, p, i)
                        if kind in "HLR":
                            continue
                        j = j0 + groups.index((kind, t))
                        u = unit(p.g + j)
                        if kind == "C":
                            ada_columns(l, p, j, 16 + 2 * t + 8 * i, i)
                        elif kind == "S":
                            dve.wait_ge(mm_done, p.g + j + 1 + i * p.groups)
                            places = score_places(l, t, u)
                            w = len(places)
                            src = u if w == 1 else u.rearrange("p (v k) -> p v k", v=2)
                            nc.vector.reduce_max(st[:, t % 3, 0:w], src[:, 0:TOK] if w == 1 else src[:, :, 0:CTX], AX.X,
                                                 negate=True).then_inc(smax, 1)
                            if t:
                                probabilities(t - 1)
                        elif kind == "T":
                            dve.wait_ge(pt_hi, after(N_TILES, l, i, t + 1))
                            src, dst = turned_places(l, t, u)
                            minus_hi(dst[1], src, dst[0]).then_inc(read_d, 1)
                            if t == N_TILES[l] - 3:
                                probabilities(t + 2)
                        elif kind == "V":
                            hd, a, _ = pv_place(l, t)
                            dve.wait_ge(o_hi, after(N_PV, l, i, t + 1))
                            minus_hi(oo[1][:, hd, a:a + 256], u[:, 0:256], oo[0][:, hd, a:a + 256]).then_inc(read_d, 1)
                    j0 += len(groups)
                    for m in range(DT):
                        dve.wait_ge(mm_done, p.g + j0 + m + 1 + i * p.groups)
                        nc.vector.tensor_tensor(tmp[m % 2][:, 0:T], unit(p.g + j0 + m)[:, 0:T], xs[:, m, 0:T], ALU.mult
                                                ).then_inc(read_d, 1)
                        dve.wait_ge(read_d, p.free_at[j0 + m][1] + i * p.dd)
                        nc.vector.tensor_tensor(ys[:, m, 0:T], ys[:, m, 0:T], tmp[m % 2][:, 0:T], ALU.add
                                                ).then_inc(merged_add, 1)
                for k in range(DT):
                    dve.wait_ge(mg_hi, DT * l + k + 1)
                    minus_hi(mg[1][:, k, 0:T], ys[:, k, 0:T], mg[0][:, k, 0:T]).then_inc(mg_lo, 1)
                gains(l, (1, 2, 3))
                p = ph["w_out", l]
                dve.wait_ge(wlo_ready, p.b + 1)
                dve.wait_ge(total_clear, 2 * l + 2)
                with dve.Fori(0, p.turns) as i:
                    for s in range(2):
                        split(p.b + s + 1, p, i)
                        for j in (2 * s, 2 * s + 1):
                            add_row(("post_mix", l), j, i, p.groups)
                dve.wait_ge(mods_step, 2 * l + 2)
                dve.wait_ge(x_back, 16 * (l + 1))
                p = ph["ff_first", l]
                residual(("post_mix", l), lambda: split(p.b + 1, p))
                stats(("pre_ffn", l))
                norm(("pre_ffn", l), xs, h[1], h[0])

                def times_up(p, j, n, i=0):
                    for m in range(2):
                        dve.wait_ge(silu_done, n + m + 1 + 4 * i)
                        dve.wait_ge(mm_done, p.g + j + m + 1 + i * p.groups)
                        nc.vector.tensor_tensor(tmp[3 + m][:, 0:T], unit(p.g + j + m)[:, 0:T], tmp[m][:, 0:T],
                                                ALU.mult).then_inc(read_d, 1)

                def hidden_lo(s, n, i=0):
                    for m in range(2):
                        dve.wait_ge(hid_hi, n + m + 1 + 4 * i)
                        minus_hi(hid[s][1][:, m, 0:T], tmp[3 + m][:, 0:T], hid[s][0][:, m, 0:T]).then_inc(hid_lo, 1)

                def add_y(p, j, m, i=0):
                    dve.wait_ge(mm_done, p.g + j + m + 1 + i * p.groups)
                    nc.vector.tensor_tensor(ys[:, m, 0:T], unit(p.g + j + m)[:, 0:T], ys[:, m, 0:T], ALU.add
                                            ).then_inc(read_d, 1)

                n0 = 2 * FF_GROUPS * l
                p = ph["ff_first", l]
                split(p.b + 2, p)
                times_up(p, 2, n0)
                hidden_lo(0, n0)
                dve.wait_ge(y_clear, l + 1)
                for p, with_ada, before in ff_phases(l):
                    with dve.Fori(0, p.turns) as i:
                        for s in range(2):
                            j, n = p.groups // 2 * s, n0 + 2 + 2 * s + 4 * before
                            split(p.b + 3 * s + 1, p, i)
                            split(p.b + 3 * s + 2, p, i)
                            times_up(p, j + 2, n, i)
                            hidden_lo(1 - s, n, i)
                            for m in range(DT):
                                if m == DT // 2:
                                    split(p.b + 3 * s + 3, p, i)
                                add_y(p, j + 4 + with_ada, m, i)
                            if with_ada:
                                ada_columns(l + 1, p, j + 13, 4 * i + 2 * s, i)
                    if with_ada:
                        dve.wait_ge(read_d, p.rd + p.turns * p.dd)
                        gains(l + 1, (0,))
                p = ph["ff_last", l]
                if l + 1 < DEPTH:
                    split(p.b + 1, p)
                dve.wait_ge(total_clear, 2 * l + 3)
                for m in range(DT):
                    add_y(p, 0, m)
                    if m:
                        add_row(("post_ffn", l), m - 1)
                add_row(("post_ffn", l), DT - 1)
                residual(("post_ffn", l))
            p = ph["out"]
            for t in (1, 3):
                dve.wait_ge(mm_done, p.g + t + 1)
                nc.vector.tensor_copy(rows[:, t, :], unit(p.g + t)[:, 0:D_MODEL]).then_inc(read_d, 1)

        @block.tensor
        def _(pe):
            def product(g, weights, moving, n_k, n_tok, ready=None):
                for a, b in segs(n_tok):
                    for k in range(n_k):
                        if ready and a == 0:
                            ready(k)
                        (wh, wl), (mh, ml) = weights(k), moving(k, a, b)
                        out_u = unit(g)[:, a:b]
                        nc.tensor.matmul(out_u, wh, mh, start=k == 0, stop=False)
                        nc.tensor.matmul(out_u, wh, ml, start=False, stop=False)
                        last = nc.tensor.matmul(out_u, wl, mh, start=False, stop=k == n_k - 1)
                return last

            def take(p, j, i=0):
                e, n = freed(p, j, i) if (p.turns > 1 or j >= 4) else (None, None)
                if e is not None:
                    pe.wait_ge(e, n)

            def drained(p):
                if p.ra:
                    pe.wait_ge(read_a, p.ra)
                if p.rd:
                    pe.wait_ge(read_d, p.rd)

            def free(g):
                e, n = plan.free_counts[g - 4]
                pe.wait_ge(read_a if e == "A" else read_d, n)

            def have(b, p, i=0):
                pe.wait_ge(wlo_ready, b + 1 + i * p.blocks)

            def cols(b, k, width, m, n=P):
                a = k * width + m
                return w_hi[:, b % 2, a:a + n], w_lo[:, b % 2, a:a + n]

            def both(x2, k, a, b):
                return x2[0][:, k, a:b], x2[1][:, k, a:b]

            def sums(key):
                n, total = plan.norms[key], slots_of(key)[1]
                pe.wait_ge(sq_done, n["sq"] + n["nk"])
                adds = 0 if key[0] == "kv" else n["nk"] - 1 if key[0] == "q" or shared(key) else n["nk"]
                if adds:
                    pe.wait_ge(sq_added, n["adds"] + adds)
                for t in range(n["T"] // P):
                    last = nc.tensor.matmul(unit(n["at"][0][0])[:, t:t + 1], tmp[total][:, t * P:(t + 1) * P],
                                            ones[:, 0:1], start=True, stop=True)
                last.then_inc(mm_done, 1)

            def spread(key):
                n = plan.norms[key]
                pe.wait_ge(diag_done, n["n"] + 1)
                for a, b in segs(n["T"]):
                    last = nc.tensor.matmul(unit(n["at"][1][0])[:, a:b], ones[:], tmp[slots_of(key)[2]][:, a:b],
                                            start=True, stop=True)
                last.then_inc(mm_done, 1)

            def stats(key):
                free(plan.norms[key]["at"][0][0])
                sums(key)
                free(plan.norms[key]["at"][1][0])
                spread(key)

            def normed(key):
                n = plan.norms[key]

                def ready(k):
                    if k < n["nk"] - 1:
                        pe.wait_ge(n_lo, n["rest"] + k + 1)
                    else:
                        pe.wait_ge(read_d, n["at"][1][1])
                return ready

            def ada_rows(p, j, parts, i):
                take(p, j, i)
                for k in range(DT):
                    c4 = cst[:, 4 * k:4 * k + P]
                    wh, wl = (w[:, k * 256:(k + 1) * 256] for w in parts)
                    nc.tensor.matmul(unit(p.g + j)[:, 0:256], c4, wh, start=k == 0, stop=False)
                    last = nc.tensor.matmul(unit(p.g + j)[:, 0:256], c4, wl, start=False, stop=k == DT - 1)
                last.then_inc(mm_done, 1)

            def block_parts(b):
                return w_hi[:, b % 2, :], w_lo[:, b % 2, :]

            def ada_columns(p, j_rows, j, s, i):
                pe.wait_ge(read_a, p.free_at[j_rows][1] + i * p.da)
                take(p, j, i)
                for m in range(2):
                    last = nc.tensor.matmul(unit(p.g + j)[:, 2 * m:2 * m + 2], mrow[:, s % 2, m * P:(m + 1) * P],
                                            pair_sum[:], start=True, stop=True)
                last.then_inc(mm_done, 1)

            def rows_block(b, p, j, moving, n_tok, ready, i=0):
                have(b, p, i)
                for m in range(2):
                    take(p, j + m, i)
                for k in range(DT):
                    ready(k)
                    for m in range(2):
                        wh, wl = cols(b, k, 256, m * P)
                        for a, e in segs(n_tok):
                            mh, ml = moving(k, a, e)
                            o = unit(p.g + j + m)[:, a:e]
                            nc.tensor.matmul(o, wh, mh, start=k == 0, stop=False)
                            nc.tensor.matmul(o, wh, ml, start=False, stop=False)
                            last = nc.tensor.matmul(o, wl, mh, start=False, stop=k == DT - 1)
                        if k == DT - 1:
                            last.then_inc(mm_done, 1)

            def full_block(b, p, j, moving, n_tok, i=0, ready=None, width=256, tiles=2, n_k=DT):
                have(b, p, i)
                for m in range(tiles):
                    take(p, j + m, i)
                    product(p.g + j + m, lambda k: cols(b, k, width, m * P), moving, n_k, n_tok,
                            ready if m == 0 else None).then_inc(mm_done, 1)

            pe.wait_ge(ident_in, 16)
            pe.wait_ge(rows_in, 16 * len(VEC_ROWS) * DEPTH)
            for l in range(DEPTH):
                nc.tensor.transpose(unit(l)[:, 0:n_vec], vrow[l][0:n_vec, :], ident[0:n_vec, 0:n_vec]
                                    ).then_inc(mm_done, 1)
            pe.wait_ge(c_ready, 4)
            pe.wait_ge(cleared, 4)
            pe.wait_ge(pair_in, 16)
            p = ph["ada_first", 0]
            for s in range(2):
                have(s, p)
                ada_rows(p, s, block_parts(s), 0)
            for s in range(2):
                ada_columns(p, s, 2 + s, s, 0)
            p = ph["x_in"]
            pe.wait_ge(x_in, 16 * (TOK // P))
            drained(p)
            for k in range(DT):
                take(p, k)
                for t in range(TOK // P):
                    last = nc.tensor.transpose(unit(p.g + k)[:, t * P:(t + 1) * P], rows[:, t, k * P:(k + 1) * P],
                                               ident[:])
                last.then_inc(mm_done, 1)
            free(plan.norms["pre_mix", 0]["at"][0][0])
            for l in range(DEPTH):
                T = tokens(l)
                if l == 0:
                    sums(("pre_mix", l))
                    p = ph["ada", l]
                    drained(p)
                    with pe.Fori(0, p.turns) as i:
                        for s in range(2):
                            have(p.b + s, p, i)
                            ada_rows(p, s, block_parts(p.b + s), i)
                        for s in range(2):
                            ada_columns(p, s, 2 + s, s, i)
                if l:
                    stats(("pre_mix", l))
                else:
                    free(plan.norms["pre_mix", l]["at"][1][0])
                    spread(("pre_mix", l))

                def hs(k, a, b):
                    return both(h, k, a, b)
                p = ph["u", l]
                drained_rows = normed(("pre_mix", l))
                rows_block(p.b, p, 0, hs, T, drained_rows)
                full_block(p.b + 1, p, 2, hs, T)
                p = ph["qkv", l]
                drained(p)
                full_block(p.b, p, 0, hs, T)
                full_block(p.b + 1, p, 2, hs, TOK, width=128, tiles=1)
                have(p.b + 2, p)
                for m in range(2):
                    take(p, 3 + m)
                    if m == 1:
                        pe.wait_ge(swap_hi, 1 + l * (PAIRS + 1))
                        pe.wait_ge(swap_lo, 1 + l * (PAIRS + 1))
                    product(p.g + 3 + m, lambda k: cols(p.b + 2, k, 256, m * P), hs, DT, TOK).then_inc(mm_done, 1)
                for half in range(2):
                    if half == 1:
                        drained(ph["sums", l])
                        sums(("q", l))
                        sums(("kv", l))
                    p = ph["g%d" % half, l]
                    drained(p)
                    with pe.Fori(0, p.turns) as i:
                        for s in range(2):
                            full_block(p.b + s, p, 2 * s, hs, T, i)
                p = ph["w_pool", l]
                drained(p)
                have(p.b, p)
                pe.wait_ge(pd_lo, NG * (l + 1))
                for g in range(NG):
                    product(p.g + g, lambda k: cols(p.b, g, P, 0), lambda k, a, b: both(pd, g, a, b), 1, T
                            ).then_inc(mm_done, 1)
                p = ph["w_o_pool", l]
                drained(p)
                for s in range(2):
                    if s == 1:
                        for n in range(2):
                            take(p, 4 + n)
                            spread((("q", "kv")[n], l))
                    full_block(p.b + s, p, 6 * s, lambda k, a, b: both(pd, k, a, b), T, width=512, tiles=4, n_k=4)
                p = ph["pairs", l]
                drained(p)
                with pe.Fori(0, p.turns) as i:
                    b0 = p.b % 2
                    have(p.b, p, i)
                    for hd in range(2):
                        take(p, hd, i)
                        product(p.g + hd, lambda k: cols(b0, k, 384, hd * (NOPE + ROPE)),
                                lambda k, a, b: both(ql, k, a, b), 2, T).then_inc(mm_done, 1)

                    for hd in range(2):
                        take(p, 2 + hd, i)
                        product(p.g + 2 + hd, lambda k: cols(b0, 0, 0, 768 + hd * 256),
                                lambda k, a, b: both(kvl, 0, a, b), 1, TOK).then_inc(mm_done, 1)
                    take(p, 4, i)
                    pe.wait_ge(swap_hi, 2 + l * (PAIRS + 1) + i)
                    pe.wait_ge(swap_lo, 2 + l * (PAIRS + 1) + i)
                    product(p.g + 4, lambda k: cols(b0, k, P, 1280), lambda k, a, b: both(ql, k, a, b), 2, T).then_inc(mm_done, 1)
                    take(p, 5, i)
                    product(p.g + 5, lambda k: cols(b0, k, P, 1536), lambda k, a, b: both(ql, k, a, b), 2, T
                            ).then_inc(mm_done, 1)
                    wv = [w[:, b0, 768:1280].rearrange("p (h n) -> p h n", h=2)[:, :, NOPE:] for w in (w_hi, w_lo)]
                    for j, (t0, t1) in enumerate(V_TILES[l]):
                        take(p, 6 + j, i)
                        for t in range(t0, t1):
                            o_v = unit(p.g + 6 + j)[:, (t - t0) * 256:(t - t0 + 1) * 256]
                            kh, kl = (kvl[n][:, 0, t * P:(t + 1) * P] for n in range(2))
                            nc.tensor.matmul(o_v, kh, wv[0], start=True, stop=False)
                            nc.tensor.matmul(o_v, kh, wv[1], start=False, stop=False)
                            last = nc.tensor.matmul(o_v, kl, wv[0], start=False, stop=True)
                        last.then_inc(mm_done, 1)
                    j0 = 6 + len(V_TILES[l])
                    tiles, sets, groups = attention_tiles(l), pv_sets(l), attention_groups(l)
                    for j, (kind, t) in enumerate(groups, j0):
                        if kind == "R":
                            have(p.b + 1 + t, p, i)
                            ada_rows(p, j, block_parts(p.b + 1 + t), i)
                            continue
                        if kind == "C":
                            ada_columns(p, j0 + groups.index(("R", t)), j, t, i)
                            continue
                        u = unit(p.g + j)
                        take(p, j, i)
                        if kind == "S":
                            if t == 0:
                                pe.wait_ge(rope_lo, 2 + l * (PAIRS + 1) + i)
                                pe.wait_ge(read_d, p.free_at[j0 - 1][1] + i * p.dd)
                            hd, m, of_ctx = tiles[t]
                            todo = ([(SEQ + v * P, v * SEQ, SEQ, TOK) for v in range(2)] if of_ctx else
                                    [(m * P, a, a, b) for a, b in segs(TOK)])
                            r = slice(hd * ROPE, (hd + 1) * ROPE)
                            for q0, o0, k0, k1 in todo:
                                o_s = u[:, o0:o0 + k1 - k0]
                                qh, qlo = (qn[n2][:, hd, q0:q0 + P] for n2 in range(2))
                                kh, klo = (kn[n2][:, hd, k0:k1] for n2 in range(2))
                                nc.tensor.matmul(o_s, qh, kh, start=True, stop=False)
                                nc.tensor.matmul(o_s, qh, klo, start=False, stop=False)
                                nc.tensor.matmul(o_s, qlo, kh, start=False, stop=False)
                                qh, qlo = (qr[n2][r, 0, q0:q0 + P] for n2 in range(2))
                                kh, klo = (kr[n2][r, 0, k0:k1] for n2 in range(2))
                                nc.tensor.matmul(o_s, qh, kh, start=False, stop=False)
                                nc.tensor.matmul(o_s, qh, klo, start=False, stop=False)
                                last = nc.tensor.matmul(o_s, qlo, kh, start=False, stop=True)
                        elif kind == "T":
                            pe.wait_ge(p_norm, after(N_STAT, l, i, 2 * t + 2))
                            e = tmp[2 + t % 3]
                            if tiles[t][2]:
                                todo = [(k * CTX + v * P, v * CTX + k * P) for v in range(2) for k in range(2)]
                            else:
                                todo = [(k * P, k * P) for k in range(KT_ALL)]
                            for o0, e0 in todo:
                                last = nc.tensor.transpose(u[:, o0:o0 + P], e[:, e0:e0 + P], ident[:])
                        else:
                            own = next(o for k, o in sets.values() if k == t)
                            turned = j0 + groups.index(("T", own[-1]))
                            pe.wait_ge(read_d, p.free_at[turned][1] + i * p.dd)
                            hd, _, k0 = pv_place(l, t)
                            n_k = KT_ALL - k0
                            for k in range(n_k):
                                vh, vl = (vv[n2][:, k0 + k, hd * V_DIM:(hd + 1) * V_DIM] for n2 in range(2))
                                ph_, pl = (pt[t % 2][n2][:, k, :] for n2 in range(2))
                                nc.tensor.matmul(u[:, 0:256], vh, ph_, start=k == 0, stop=False)
                                nc.tensor.matmul(u[:, 0:256], vh, pl, start=False, stop=False)
                                last = nc.tensor.matmul(u[:, 0:256], vl, ph_, start=False, stop=k == n_k - 1)
                        last.then_inc(mm_done, 1)
                    last_v = j0 + groups.index(("V", len(sets) - 1))
                    pe.wait_ge(read_d, p.free_at[last_v][1] + i * p.dd)
                    full_block(p.b + 5, p, j0 + len(groups), lambda k, a, b: both(oo, k, a, b), T, i, width=D_MODEL,
                               tiles=DT, n_k=2)
                p = ph["w_out", l]
                drained(p)
                with pe.Fori(0, p.turns) as i:
                    rows_block(p.b, p, 0, lambda k, a, b: both(mg, k, a, b), T,
                               lambda k: pe.wait_ge(mg_lo, DT * l + k + 1), i)
                    full_block(p.b + 1, p, 2, lambda k, a, b: both(mg, k, a, b), T, i)
                stats(("post_mix", l))
                stats(("pre_ffn", l))
                p = ph["ff_first", l]
                rows_ready = normed(("pre_ffn", l))
                rows_block(p.b, p, 0, hs, T, rows_ready)
                full_block(p.b + 1, p, 2, hs, T)
                n0 = 2 * FF_GROUPS * l

                def down(b, p, j, s, i=0):
                    full_block(b, p, j, lambda k, a, b: both(hid[s], k, a, b), T, i, width=D_MODEL, tiles=DT, n_k=2)
                for p, with_ada, before in ff_phases(l):
                    drained(p)
                    with pe.Fori(0, p.turns) as i:
                        for s in range(2):
                            j = p.groups // 2 * s
                            full_block(p.b + 3 * s, p, j, hs, T, i)
                            full_block(p.b + 3 * s + 1, p, j + 2, hs, T, i)
                            if with_ada:
                                pe.wait_ge(ada_lo_ready, 2 * i + (s + 1))
                                ada_rows(p, j + 4, (ada_hi, ada_lo), i)
                            pe.wait_ge(hid_lo, n0 + 2 + 2 * s + 4 * before + 4 * i)
                            down(p.b + 3 * s + 2, p, j + 4 + with_ada, s, i)
                            if with_ada:
                                ada_columns(p, j + 4, j + 13, s, i)
                p = ph["ff_last", l]
                drained(p)
                pe.wait_ge(hid_lo, n0 + 2 * FF_GROUPS)
                down(p.b, p, 0, 0)
                stats(("post_ffn", l))
            p = ph["out"]
            for own in ((0, 1, 2), (3,)):
                for t in own:
                    free(p.g + t)
                for k in range(DT):
                    updated(pe, ("post_ffn", DEPTH - 1), k)
                    for t in own:
                        last = nc.tensor.transpose(unit(p.g + t)[:, k * P:(k + 1) * P], xs[:, k, t * P:(t + 1) * P],
                                                   ident[:])
                        if k == DT - 1:
                            last.then_inc(mm_done, 1)


_INS = ['x', 'c', 'ctx', 'c_ctx', 'w_ada', 'b_ada', 'g_pre_mix', 'w_in', 'q_norm', 'w_uq', 'kv_norm', 'w_ukv',
        'w_o_mla', 'w_pool', 'pool_scale', 'w_o_pool', 'w_out', 'g_post_mix', 'g_pre_ffn', 'w_ffn_gate',
        'w_ffn_up', 'w_ffn_down', 'g_post_ffn']
_OUTS = [((1, 512, 1024), 'float32')]


def shape_constants():
    import numpy as np
    ident = np.eye(P, dtype=np.float32)
    pos = np.stack([np.arange(SEQ) // GRID_W, np.arange(SEQ) % GRID_W]).astype(np.float32)
    axis = ROPE // 2
    freq = np.float32(THETA) ** (-np.arange(0, axis, 2, dtype=np.float32) / np.float32(axis))
    ang = (pos[:, None, :] * freq[None, :, None]).astype(np.float32)
    cos, sin = np.cos(ang), np.sin(ang)
    cos = np.stack([cos, cos], 1).reshape(ROPE, SEQ)
    sin = np.stack([-sin, sin], 1).reshape(ROPE, SEQ)
    rope = np.stack([np.tile(cos, (2, 1)), np.tile(sin, (2, 1))], 1).astype(np.float32)
    edge = np.ones((NG, 2, 2, PAD), np.float32)
    for g, w in enumerate(WINDOWS):
        for t, n in enumerate((SEQ, CTX)):
            q = np.arange(n)
            count = np.clip(q + w - w // 2, 0, n) - np.clip(q - w // 2, 0, n)
            edge[g, 0, t], edge[g, 1, t] = w / count[:PAD], w / count[-PAD:]
    edge = np.ascontiguousarray(np.broadcast_to(edge, (P,) + edge.shape))
    pair = np.array([[1, 0], [1, 0], [0, 1], [0, 1]], np.float32)
    return {"k_ident": ident, "k_rope": rope, "k_edge": edge, "k_pair": pair}


def kernel(**inputs):
    import numpy as _np
    import concourse.bacc as _bacc
    from concourse import mybir as _mybir
    from concourse.bass_utils import run_bass_kernel_spmd as _run

    nc = _bacc.Bacc("TRN2", target_bir_lowering=False, num_devices=1, dynamic_dma_scratch_size=256)
    arrays, args = {}, []
    consts = shape_constants()
    for name in _INS + list(consts):
        a = _np.ascontiguousarray(inputs[name] if name in inputs else consts[name])
        arrays[f"in_{name}_dram"] = a
        args.append(nc.dram_tensor(f"in_{name}_dram", a.shape, _mybir.dt.from_np(a.dtype), kind="ExternalInput").ap())
    for i, (shape, dtype) in enumerate(_OUTS):
        dt = _mybir.dt.from_np(_np.dtype(dtype))
        args.append(nc.dram_tensor(f"out_{i}_dram", shape, dt, kind="ExternalOutput").ap())
    args.append(nc.dram_tensor("x_keep", (P, DT, TOK), _mybir.dt.float32, kind="Internal").ap())
    backbone_kernel(nc, *args)
    r = _run(nc, [arrays], core_ids=[0])
    got = tuple(r.results[0][f"out_{i}_dram"] for i in range(len(_OUTS)))
    return got[0]
```
